# Optimizing a Trainium2 kernel written in Bass

```python
import math
import jax, jax.numpy as jnp
from jax import lax
import numpy as np

D_MODEL = 1024
BATCH = 1
SEQ = 512
DEPTH = 1

HEAD_DIM = 64
H_A = 4
H_B = 4
H_C = 4
KV_C = 2
H_D = 4
N_MIXERS = 4
D_MIX = HEAD_DIM * (H_A + H_B + H_C + H_D)
N_IN = 3 * HEAD_DIM * H_A + 3 * HEAD_DIM * H_B + HEAD_DIM * (H_C + 2 * KV_C) + 3 * HEAD_DIM * H_D + H_D
DILATED_GROUPS = ((128, 1), (512, 4), (2048, 16))
BAND_BLOCK = 128
MOBA_BLOCK = 256
MOBA_TOPK = 3
MOBA_Q_CHUNK = 128
SWA_WINDOW = 128
FOX_Q_BLOCK = 128
N_BUCKETS = 32
T5_MAX_DISTANCE = 2048
N_BIAS_HEADS = H_A + H_B + H_C
D_FF = -(-(8 * D_MODEL) // (3 * 256)) * 256
EPS = 1e-6
NEG = -1e30
SCALE = HEAD_DIM ** -0.5

kernel_name = 'hybrid_parallel_heads_dilated_moba_swa_fox'

def rmsnorm(x, g):
    xf = x.astype(jnp.float32)
    y = xf * lax.rsqrt(jnp.mean(xf * xf, axis=-1, keepdims=True) + EPS)
    return (y * g.astype(jnp.float32)).astype(x.dtype)

def group_rmsnorm(y, g):
    B, S, _ = y.shape
    yg = y.reshape(B, S, N_MIXERS, D_MIX // N_MIXERS)
    return rmsnorm(yg, g.reshape(N_MIXERS, D_MIX // N_MIXERS)).reshape(B, S, D_MIX)

def t5_bucket(dist):
    n = jnp.maximum(dist, 0)
    max_exact = N_BUCKETS // 2
    nf = jnp.maximum(n, 1).astype(jnp.float32)
    large = max_exact + (jnp.log(nf / max_exact) / math.log(T5_MAX_DISTANCE / max_exact)
                         * (N_BUCKETS - max_exact)).astype(jnp.int32)
    large = jnp.minimum(large, N_BUCKETS - 1)
    return jnp.where(n < max_exact, n, large)

def band_bias(table, step):
    i = jnp.arange(BAND_BLOCK)[:, None]
    j = jnp.arange(2 * BAND_BLOCK)[None, :]
    b = t5_bucket((i + BAND_BLOCK - j) * step)
    return jnp.transpose(table[b], (2, 0, 1))

def to_heads(t, h):
    B, S, _ = t.shape
    return t.reshape(B, S, h, HEAD_DIM).transpose(0, 2, 1, 3)

def from_heads(o):
    B, H, S, D = o.shape
    return o.transpose(0, 2, 1, 3).reshape(B, S, H * D)

def banded_attn(q, k, v, max_dist, bias, sink):
    B, G, R, L, D = q.shape
    n = -(-L // BAND_BLOCK)
    pad = n * BAND_BLOCK - L
    q = jnp.pad(q, ((0, 0), (0, 0), (0, 0), (0, pad), (0, 0)))
    k = jnp.pad(k, ((0, 0), (0, 0), (0, pad), (0, 0)))
    v = jnp.pad(v, ((0, 0), (0, 0), (0, pad), (0, 0)))
    qb = q.reshape(B, G, R, n, BAND_BLOCK, D)
    kb = k.reshape(B, G, n, BAND_BLOCK, D)
    vb = v.reshape(B, G, n, BAND_BLOCK, D)
    shift = ((0, 0), (0, 0), (1, 0), (0, 0), (0, 0))
    kw = jnp.concatenate([jnp.pad(kb, shift)[:, :, :n], kb], axis=3)
    vw = jnp.concatenate([jnp.pad(vb, shift)[:, :, :n], vb], axis=3)
    s = jnp.einsum('bgrnqd,bgnkd->bgrnqk', qb, kw).astype(jnp.float32) * SCALE
    s = s + bias[:, :, None].astype(jnp.float32)
    i = jnp.arange(BAND_BLOCK)[:, None]
    j = jnp.arange(2 * BAND_BLOCK)[None, :]
    dist = i + BAND_BLOCK - j
    in_band = (dist >= 0) & (dist <= max_dist)
    has_prev = (jnp.arange(n)[:, None, None] > 0) | (j >= BAND_BLOCK)[None]
    s = jnp.where(in_band[None] & has_prev, s, NEG)
    if sink is not None:
        sk = jnp.broadcast_to(sink.astype(jnp.float32)[None, :, :, None, None, None], s.shape[:-1] + (1,))
        s = jnp.concatenate([s, sk], axis=-1)
    lse = jax.nn.logsumexp(s, axis=-1, keepdims=True)
    p = jnp.exp(s - lse)[..., :2 * BAND_BLOCK]
    o = jnp.einsum('bgrnqk,bgnkd->bgrnqd', p.astype(v.dtype), vw)
    o = o.reshape(B, G, R, n * BAND_BLOCK, D)[:, :, :, :L]
    lse = lse[..., 0].reshape(B, G, R, n * BAND_BLOCK)[:, :, :, :L]
    return o, lse

def dilated_mixture(q, k, v, table):
    B, H, S, D = q.shape
    outs, lses = [], []
    for window, dil in DILATED_GROUPS:
        L = S // dil

        def fold(t):
            return t.reshape(B, H, L, dil, D).transpose(0, 3, 1, 2, 4).reshape(B * dil, H, L, D)

        bias = band_bias(table, dil)[:, None]
        o, lse = banded_attn(fold(q)[:, :, None], fold(k), fold(v), window // dil, bias, None)
        outs.append(o[:, :, 0].reshape(B, dil, H, L, D).transpose(0, 2, 3, 1, 4).reshape(B, H, S, D))
        lses.append(lse[:, :, 0].reshape(B, dil, H, L).transpose(0, 2, 3, 1).reshape(B, H, S))
    w = jax.nn.softmax(jnp.stack(lses), axis=0)
    return jnp.einsum('gbhs,gbhsd->bhsd', w.astype(q.dtype), jnp.stack(outs))

def moba_attn(q, k, v, table):
    B, H, S, D = q.shape
    nb = -(-S // MOBA_BLOCK)
    Sp = nb * MOBA_BLOCK
    padw = ((0, 0), (0, 0), (0, Sp - S), (0, 0))
    q, k, v = jnp.pad(q, padw), jnp.pad(k, padw), jnp.pad(v, padw)
    kb = k.reshape(B, H, nb, MOBA_BLOCK, D)
    vb = v.reshape(B, H, nb, MOBA_BLOCK, D)
    k_mean = jnp.mean(kb.astype(jnp.float32), axis=3)
    topk = min(MOBA_TOPK, nb)
    table_t = table.T
    bi = jnp.arange(B)[:, None, None, None]
    hi = jnp.arange(H)[None, :, None, None]
    blk_ids = jnp.arange(nb)
    in_blk = jnp.arange(MOBA_BLOCK)
    Q = MOBA_Q_CHUNK

    def chunk(c):
        start = c * Q
        t = start + jnp.arange(Q)
        own = start // MOBA_BLOCK
        qc = lax.dynamic_slice_in_dim(q, start, Q, axis=2)
        gate = jnp.einsum('bhqd,bhnd->bhqn', qc.astype(jnp.float32), k_mean)
        gate = jnp.where(blk_ids < own, gate, -jnp.inf)
        _, idx = lax.top_k(gate, topk)
        valid = jnp.arange(topk) < own
        k_sel = kb[bi, hi, idx]
        v_sel = vb[bi, hi, idx]
        dist_sel = t[:, None, None] - (idx[..., None] * MOBA_BLOCK + in_blk)
        bias_sel = table_t[hi[..., None], t5_bucket(dist_sel)]
        s_sel = jnp.einsum('bhqd,bhqnkd->bhqnk', qc, k_sel).astype(jnp.float32) * SCALE
        s_sel = jnp.where(valid[:, None], s_sel + bias_sel.astype(jnp.float32), NEG)
        k_own = lax.dynamic_index_in_dim(kb, own, axis=2, keepdims=False)
        v_own = lax.dynamic_index_in_dim(vb, own, axis=2, keepdims=False)
        dist_own = t[:, None] - (own * MOBA_BLOCK + in_blk)[None, :]
        s_own = jnp.einsum('bhqd,bhkd->bhqk', qc, k_own).astype(jnp.float32) * SCALE
        s_own = s_own + table_t[:, t5_bucket(dist_own)].astype(jnp.float32)
        s_own = jnp.where(dist_own >= 0, s_own, NEG)
        s = jnp.concatenate([s_sel.reshape(B, H, Q, topk * MOBA_BLOCK), s_own], axis=-1)
        p = jax.nn.softmax(s, axis=-1).astype(v.dtype)
        p_sel = p[..., :topk * MOBA_BLOCK].reshape(B, H, Q, topk, MOBA_BLOCK)
        return (jnp.einsum('bhqnk,bhqnkd->bhqd', p_sel, v_sel)
                + jnp.einsum('bhqk,bhkd->bhqd', p[..., topk * MOBA_BLOCK:], v_own))

    o = lax.map(chunk, jnp.arange(Sp // Q))
    return o.transpose(1, 2, 0, 3, 4).reshape(B, H, Sp, D)[:, :, :S]

def forgetting_attn(q, k, v, log_f):
    B, H, S, D = q.shape
    n = -(-S // FOX_Q_BLOCK)
    Sp = n * FOX_Q_BLOCK
    padw = ((0, 0), (0, 0), (0, Sp - S), (0, 0))
    q, k, v = jnp.pad(q, padw), jnp.pad(k, padw), jnp.pad(v, padw)
    c = lax.cumsum(jnp.pad(log_f, ((0, 0), (0, 0), (0, Sp - S))), axis=2)
    kpos = jnp.arange(Sp)

    def blk(i):
        start = i * FOX_Q_BLOCK
        qi = lax.dynamic_slice_in_dim(q, start, FOX_Q_BLOCK, axis=2)
        ci = lax.dynamic_slice_in_dim(c, start, FOX_Q_BLOCK, axis=2)
        s = jnp.einsum('bhqd,bhkd->bhqk', qi, k).astype(jnp.float32) * SCALE
        s = s + ci[..., None] - c[:, :, None, :]
        causal = (start + jnp.arange(FOX_Q_BLOCK))[:, None] >= kpos[None, :]
        p = jax.nn.softmax(jnp.where(causal, s, NEG), axis=-1)
        return jnp.einsum('bhqk,bhkd->bhqd', p.astype(v.dtype), v)

    o = lax.map(blk, jnp.arange(n))
    return o.transpose(1, 2, 0, 3, 4).reshape(B, H, Sp, D)[:, :, :S]

def setup_inputs(seed: int = 0) -> dict:
    key = jax.random.key(seed)
    ks = jax.random.split(key, 13)
    nrm = jax.random.normal
    return {
        'x': nrm(ks[0], (BATCH, SEQ, D_MODEL), jnp.float32),
        'norm1_g': 1.0 + 0.1 * nrm(ks[1], (DEPTH, D_MODEL), jnp.float32),
        'w_in': nrm(ks[2], (DEPTH, D_MODEL, N_IN), jnp.float32) * D_MODEL ** -0.5,
        'f_bias': 2.0 + 0.5 * nrm(ks[3], (DEPTH, H_D), jnp.float32),
        'sinks': 0.5 * nrm(ks[4], (DEPTH, H_C), jnp.float32),
        'mix_norm_g': 1.0 + 0.1 * nrm(ks[5], (DEPTH, D_MIX), jnp.float32),
        'w_out': nrm(ks[6], (DEPTH, D_MIX, D_MODEL), jnp.float32) * D_MIX ** -0.5,
        'norm2_g': 1.0 + 0.1 * nrm(ks[7], (DEPTH, D_MODEL), jnp.float32),
        'w_gate': nrm(ks[8], (DEPTH, D_MODEL, D_FF), jnp.float32) * D_MODEL ** -0.5,
        'w_up': nrm(ks[9], (DEPTH, D_MODEL, D_FF), jnp.float32) * D_MODEL ** -0.5,
        'w_down': nrm(ks[10], (DEPTH, D_FF, D_MODEL), jnp.float32) * D_FF ** -0.5,
        'rel_bias': 0.5 * nrm(ks[11], (N_BUCKETS, N_BIAS_HEADS), jnp.float32),
        'final_g': 1.0 + 0.1 * nrm(ks[12], (D_MODEL,), jnp.float32),
    }

def reference(x, norm1_g, w_in, f_bias, sinks, mix_norm_g, w_out, norm2_g, w_gate, w_up, w_down, rel_bias, final_g):
    B, S, _ = x.shape
    table_a = rel_bias[:, :H_A]
    table_b = rel_bias[:, H_A:H_A + H_B]
    table_c = rel_bias[:, H_A + H_B:]
    rep_c = H_C // KV_C
    bias_c = band_bias(table_c, 1).reshape(KV_C, rep_c, BAND_BLOCK, 2 * BAND_BLOCK)
    hd = HEAD_DIM
    sizes = [hd * H_A] * 3 + [hd * H_B] * 3 + [hd * H_C, hd * KV_C, hd * KV_C] + [hd * H_D] * 3 + [H_D]
    offsets = np.cumsum(sizes)[:-1].tolist()
    for l in range(DEPTH):
        h = rmsnorm(x, norm1_g[l])
        qa, ka, va, qb, kb, vb, qc, kc, vc, qd, kd, vd, fd = jnp.split(h @ w_in[l], offsets, axis=-1)
        o_a = dilated_mixture(to_heads(qa, H_A), to_heads(ka, H_A), to_heads(va, H_A), table_a)
        o_b = moba_attn(to_heads(qb, H_B), to_heads(kb, H_B), to_heads(vb, H_B), table_b)
        q_c = to_heads(qc, H_C).reshape(B, KV_C, rep_c, S, HEAD_DIM)
        o_c, _ = banded_attn(q_c, to_heads(kc, KV_C), to_heads(vc, KV_C), SWA_WINDOW - 1,
                             bias_c, sinks[l].reshape(KV_C, rep_c))
        o_c = o_c.reshape(B, H_C, S, HEAD_DIM)
        log_f = jax.nn.log_sigmoid((fd + f_bias[l]).astype(jnp.float32)).transpose(0, 2, 1)
        o_d = forgetting_attn(to_heads(qd, H_D), to_heads(kd, H_D), to_heads(vd, H_D), log_f)
        mix = jnp.concatenate([from_heads(o_a), from_heads(o_b), from_heads(o_c), from_heads(o_d)], axis=-1)
        x = x + group_rmsnorm(mix, mix_norm_g[l]) @ w_out[l]
        h = rmsnorm(x, norm2_g[l])
        x = x + (jax.nn.silu(h @ w_gate[l]) * (h @ w_up[l])) @ w_down[l]
    return rmsnorm(x, final_g)


_drawn_inputs = setup_inputs


def setup_inputs(seed=0):
    import zlib

    import numpy as np

    out = dict(_drawn_inputs(seed))
    spreads = {}
    factors = {'sinks': 8.0}
    for name, (base, spread) in spreads.items():
        noise = np.random.default_rng([zlib.crc32(name.encode()), seed]).standard_normal(out[name].shape)
        drawn = base * np.exp(spread * noise) if base else spread * noise
        out[name] = __import__('jax').numpy.asarray(drawn.astype(out[name].dtype))
    for name, factor in factors.items():
        out[name] = (out[name] * factor).astype(out[name].dtype)
    return out
```

```python
from contextlib import ExitStack

import numpy as np
import concourse.bass as bass
from concourse import mybir

F32 = mybir.dt.float32
F32R = mybir.dt.float32r
ALU = mybir.AluOpType
ACT = mybir.ActivationFunctionType

P = 128
SEQ = 512
D_MODEL = 1024
HEAD_DIM = 64
N_BUCKETS = 32
T5_MAX_DISTANCE = 2048
D_FF = 2816
EPS = 1e-6
NEG = -1e30
SCALE = HEAD_DIM ** -0.5
LOWEST = -3.0e38

NT = SEQ // P
NK = D_MODEL // P
FC = D_FF // P
PAIRS = 8
STEPS = 8 * PAIRS
GROUP_D, GROUP_A, GROUP_B, GROUP_C = range(4)
RAW = 4
SPLIT = 4
UNIT = NK * P
MIX_SLOTS = 6
MIX_AT = [768, 0, 256, 512]
Q_AT = [2048, 0, 768, 1536]
K_AT = [2304, 256, 1024, 1792]
V_AT = [2560, 512, 1280, 1920]
F_AT = 2816
ROW = 640
BIAS_HEADS = 12
MASK_ROW = BIAS_HEADS
PT_STRIDE = 384
PT_WIDTH = 3 * PT_STRIDE + SEQ


def group_of(pair):
    return pair // 2


def head_of(pair, side):
    c = pair % 2
    return c + 2 * side if group_of(pair) == GROUP_C else 2 * c + side


def keys_of(n):
    pair, side, i = n // 8, n // 4 % 2, n % 4
    first = P * (i - 1) if group_of(pair) == GROUP_C and i else 0
    return pair, side, i, first, P * (i + 1) - first


def kv_slot(pair):
    return pair % 2 if pair < 7 else 0


def plan():
    events, unit_job, count = [], {}, {"job": 0, "unit": 0}

    def job():
        count["job"] += 1
        return count["job"] - 1

    def norm(which):
        for t in range(NT):
            events.append(("square", which, t))
            events.append(("root", which, t))
            events.append(("scale", which, t))
            for half in range(2):
                j = job()
                events.append(("turn_h", which, t, half, j))
                events.append(("drain_h", which, t, half, j))

    def next_unit():
        u = count["unit"]
        count["unit"] += 1
        return u

    def ahead(u):
        events.append(("split", u + SPLIT - 1))
        events.append(("load", u + SPLIT - 1 + RAW))

    def projection(kind, pair):
        u, j = next_unit(), job()
        unit_job[u] = j
        for r in range(3):
            events.append(("piece", kind, u, j, r))
            if r == 1:
                ahead(u)
            yield
        events.append(("drain", kind, pair, j))

    def turn_values(pair):
        j = job()
        events.append(("turn_v", pair, j))
        yield
        events.append(("drain_v", pair, j))

    def projections(pair):
        if pair == 7:
            return projection("q", pair)
        return chain(projection("v", pair), projection("q", pair), turn_values(pair), projection("k", pair))

    def output(group, half):
        if half == 0:
            j = job()
            events.append(("stats", group, j))
            yield
            events.append(("drain_stats", group, j))
        u = next_unit()
        for t in range(NT):
            j = job()
            unit_job[u] = j
            events.append(("out", group, half, t, u, j))
            if t == 1:
                ahead(u)
            yield
            events.append(("drain_out", group, half, t, j))

    def chain(*parts):
        for part in parts:
            yield from part

    def run(filler):
        for _ in filler:
            pass

    for u in range(RAW):
        events.append(("load", u))
    for part in range(2):
        j = job()
        events.append(("table", part, j))
        events.append(("drain_table", part, j))
    events.append(("store_rows",))
    for t in range(SPLIT - 1):
        events.append(("split", t))
        events.append(("load", t + RAW))
    norm(0)
    events.append(("bias", 0))
    events.append(("bias", 1))
    run(chain(projection("f", 0), projections(0)))

    fillers = [projections(pair + 1) for pair in range(PAIRS - 1)] + [chain()]
    fillers[2] = chain(fillers[2], output(GROUP_D, 0))
    fillers[3] = chain(fillers[3], output(GROUP_D, 1))
    fillers[4] = chain(fillers[4], output(GROUP_A, 0))
    fillers[6] = chain(fillers[6], output(GROUP_A, 1))
    fillers[7] = chain(output(GROUP_B, 0))
    pieces = [10, 10, 15, 14, 15, 10, 7, 5]

    for s in range(STEPS + 5):
        pair = min(s // 8, PAIRS - 1)
        if s < STEPS:
            events.append(("scores", s))
        share = pieces[pair] / 8
        at = s % 8
        n = int(share * (at + 1) + 1e-6) - int(share * at + 1e-6) if s < STEPS else 1
        for _ in range(n - n // 2):
            next(fillers[pair], None)
        if s < STEPS:
            events.append(("max", s))
            events.append(("exp", s))
        if 0 <= s - 1 < STEPS:
            events.append(("norm", s - 1))
        if 0 <= s - 2 < STEPS:
            events.append(("turn", s - 2))
            events.append(("keep", s - 2))
        for _ in range(n // 2):
            next(fillers[pair], None)
        if s >= 6 and (s - 6) % 4 == 0 and (s - 6) // 4 < 2 * PAIRS:
            events.append(("values", (s - 6) // 4))
        if s >= 7 and (s - 7) % 4 == 0:
            events.append(("gather", (s - 7) // 4))
        if s % 8 == 7:
            run(fillers[pair])
            if 2 <= pair + 1 < PAIRS:
                events.append(("bias", pair + 1))
        if s == STEPS:
            fillers[-1] = output(GROUP_B, 1)
    run(fillers[-1])
    run(chain(output(GROUP_C, 0), output(GROUP_C, 1)))
    norm(1)
    return events, unit_job, count["job"], count["unit"]


def band_constants():
    dist = SEQ - 1 - np.arange(ROW)
    n = np.maximum(dist, 0)
    exact = N_BUCKETS // 2
    large = exact + (np.log(np.maximum(n, 1) / exact) / np.log(T5_MAX_DISTANCE / exact)
                     * (N_BUCKETS - exact)).astype(np.int64)
    bucket = np.where(n < exact, n, np.minimum(large, N_BUCKETS - 1))
    onehot = (np.arange(N_BUCKETS)[:, None] == bucket).astype(np.float32)
    causal = dist >= 0
    bands = (dist <= 128).astype(int) + (dist % 4 == 0) + (dist % 16 == 0)
    add = np.zeros((BIAS_HEADS + 1, ROW), np.float32)
    add[0:4] = np.where(causal & (bands > 0), np.log(np.maximum(bands, 1)), NEG)
    add[4:8] = np.where(causal, 0.0, NEG)
    add[8:12] = np.where(causal & (dist < 128), 0.0, NEG)
    add[MASK_ROW] = np.where(causal, 0.0, NEG)
    pick = np.zeros((P, 4, P), np.float32)
    for h in range(4):
        pick[h::32, h] = 1.0
    return onehot, add, pick


def hybrid_layer(nc, x, units, gains, mix_gain, f_bias, sinks, rel_bias, onehot, band_add, pick, out):
    EVENTS, UNIT_JOB, JOBS, U_MLP = plan()
    U_DOWN = U_MLP + 2 * FC
    N_UNITS = U_DOWN + FC
    HEADS = 2 * PAIRS
    hi_upto, job_of, job_at, hi_count = {}, {}, {}, 0
    for e in EVENTS:
        if e[0] == "drain_h" or e[0] == "drain_v" or (e[0] == "drain" and e[1] in "qk"):
            hi_count += 1
            hi_upto[e[-1]] = hi_count
        if e[0] == "drain":
            job_of[e[1], e[2]] = e[3]
        if e[0] == "drain_v":
            job_of["v_turned", e[1]] = e[2]
        if e[0] == "drain_h":
            job_of["h", e[1]] = e[4]
            job_at["h", e[1], e[2]] = e[4]
        if e[0] == "stats":
            job_of["stats", e[1]] = e[2]
        if e[0] == "out":
            job_of["out", e[1], e[2], e[3]] = e[5]
    for what in ("k", "v", "v_turned"):
        job_of[what, 7] = job_of[what, 6]

    bias_rows = nc.dram_tensor("bias_rows", (BIAS_HEADS, ROW), F32, kind="Internal")

    def skewed(rows, row, step):
        return bass.AP(tensor=rows, offset=row * ROW, ap=[[1, P], [step * ROW, 2], [1, SEQ]])

    with ExitStack() as ctx:
        def sb(name, shape, dt=F32, stack=ctx):
            return stack.enter_context(nc.sbuf_tensor(name, shape, dt))

        def sem(name):
            return ctx.enter_context(nc.semaphore(name))

        xs = sb("xs", [P, NT, D_MODEL])
        h_hi = sb("h_hi", [P, NK, SEQ], F32R)
        h_lo = sb("h_lo", [P, NK, SEQ], F32R)
        raw = sb("raw", [P, RAW, UNIT])
        w_hi = sb("w_hi", [P, SPLIT, UNIT], F32R)
        w_lo = sb("w_lo", [P, SPLIT, UNIT], F32R)
        gain = sb("gain", [P, D_MODEL])
        ident = sb("ident", [P, P])
        mirror = sb("mirror", [P, P])
        ones = sb("ones", [P, P])
        table = sb("table", [N_BUCKETS, BIAS_HEADS])
        mix_g = sb("mix_g", [P, PAIRS])
        fb = sb("fb", [4, 1])
        sink = sb("sink", [P, 4])
        minus_half = sb("minus_half", [P, NT])
        zero_row = sb("zero_row", [4, SEQ])
        ssq = sb("ssq", [P, 3, NT])
        mean = sb("mean", [P, 3, NT])
        rstd = sb("rstd", [P, 3, NT])
        g_mean = sb("g_mean", [P, 4, NT])
        g_rstd = sb("g_rstd", [P, 4, NT])
        top = sb("top", [P, STEPS])
        shift = sb("shift", [P, STEPS])
        total = sb("total", [P, STEPS])
        sink_e = sb("sink_e", [P, STEPS])
        total2 = sb("total2", [P, STEPS])
        inv = sb("inv", [P, STEPS])
        tb = sb("tb", [P, 2, 1024])
        attn = ctx.enter_context(ExitStack())
        q_hi = sb("q_hi", [P, 2, SEQ], F32R, attn)
        q_lo = sb("q_lo", [P, 2, SEQ], F32R, attn)
        k_hi = sb("k_hi", [P, 2, SEQ], F32R, attn)
        k_lo = sb("k_lo", [P, 2, SEQ], F32R, attn)
        v_hi = sb("v_hi", [P, 2, NT, P], F32R, attn)
        v_lo = sb("v_lo", [P, 2, NT, P], F32R, attn)
        pt_hi = sb("pt_hi", [P, 2, PT_WIDTH], F32R, attn)
        pt_lo = sb("pt_lo", [P, 2, PT_WIDTH], F32R, attn)
        mix_hi = sb("mix_hi", [P, MIX_SLOTS, SEQ], F32R, attn)
        mix_lo = sb("mix_lo", [P, MIX_SLOTS, SEQ], F32R, attn)
        decay = sb("decay", [P, SEQ], F32R, attn)
        pick_r = sb("pick_r", [P, 4, P], F32R, attn)
        pick_f = sb("pick_f", [P, 4, P], F32, attn)
        s_buf = sb("s_buf", [P, 3, SEQ], F32, attn)
        sq = sb("sq", [P, 2, SEQ], F32, attn)
        vt = sb("vt", [P, 2, SEQ], F32, attn)
        attn.close()
        mlp = ctx.enter_context(ExitStack())
        gu_hi = sb("gu_hi", [P, FC, SEQ], F32R, mlp)
        gu_lo = sb("gu_lo", [P, FC, SEQ], F32R, mlp)
        act_g, gated = tb[:, :, 0:SEQ], tb[:, :, SEQ:2 * SEQ]
        hot = sq[0:N_BUCKETS, :, :].rearrange("p a b -> p (a b)")[:, 0:ROW]
        rows = vt[0:BIAS_HEADS, :, :].rearrange("p a b -> p (a b)")[:, 0:ROW]

        ps = ctx.enter_context(nc.psum_tensor("ps", [P, 8, SEQ], F32))
        PROJ, SCORE, TURN, VALUE = 0, 2, 4, 6

        x_landed = [sem(f"x_landed{t}") for t in range(NT)]
        gain_landed = sem("gain_landed")
        const_landed = sem("const_landed")
        table_landed = sem("table_landed")
        rows_stored = sem("rows_stored")
        bias_landed = [sem(f"bias_landed{i}") for i in range(2)]
        raw_landed = [sem(f"raw_landed{i}") for i in range(RAW)]
        out_stored = sem("out_stored")
        consts_ready = sem("consts_ready")
        squared = sem("squared")
        mean_ready = sem("mean_ready")
        rstd_ready = sem("rstd_ready")
        scaled = sem("scaled")
        job_done = sem("job_done")
        job_hi = sem("job_hi")
        bank_drained = sem("bank_drained")
        split_hi = sem("split_hi")
        split_lo = sem("split_lo")
        decay_step = sem("decay_step")
        softplus_ready = sem("softplus_ready")
        scores_ready = sem("scores_ready")
        top_ready = sem("top_ready")
        shift_ready = sem("shift_ready")
        exp_ready = sem("exp_ready")
        sink_ready = sem("sink_ready")
        total_ready = sem("total_ready")
        inv_ready = sem("inv_ready")
        probs_ready = sem("probs_ready")
        turned = sem("turned")
        kept_hi = sem("kept_hi")
        kept_lo = sem("kept_lo")
        values_ready = sem("values_ready")
        gathered_hi = sem("gathered_hi")
        gathered_lo = sem("gathered_lo")
        zeros_ready = sem("zeros_ready")
        g_rstd_ready = sem("g_rstd_ready")
        silu_ready = sem("silu_ready")
        gu_hi_ready = sem("gu_hi_ready")
        gu_lo_ready = sem("gu_lo_ready")
        down_done = sem("down_done")
        added = sem("added")

        def as_f32(ap):
            return ap.bitcast(F32)

        def landed(eng, u):
            eng.wait_ge(raw_landed[u % RAW], 16 * (u // RAW + 1))

        def pt_blocks(buf, n):
            _, _, i, first, width = keys_of(n)
            j0, nj = first // P, width // P
            at = P * i + PT_STRIDE * j0
            slot = buf[:, n // 4 % 2, :]
            return bass.AP(tensor=slot.tensor, offset=slot.offset + at, ap=[list(slot.ap[0]), [PT_STRIDE, nj], [1, P]])

        def projected(kind, j):
            bank = ps[:, PROJ + j % 2, :]
            if kind == "q":
                return bass.AP(tensor=bank.tensor, offset=bank.offset + P - 1, ap=[list(bank.ap[0]), [P, NT], [-1, P]])
            return bank.rearrange("p (t c) -> p t c", c=P)

        def by_tiles(ap):
            return ap.rearrange("p (t c) -> p t c", c=P)

        def every_row(which):
            return bass.AP(tensor=gains.tensor, offset=which * D_MODEL, ap=[[0, P], [1, D_MODEL]])

        block = ctx.enter_context(nc.Block())

        @block.sync
        def _(sp):
            sp.dma_start(xs[:, 0, :], x[0:P, :]).then_inc(x_landed[0], 16)
            sp.dma_start(gain[:], every_row(0)).then_inc(gain_landed, 16)
            for t in range(1, NT):
                sp.dma_start(xs[:, t, :], x[t * P:(t + 1) * P, :]).then_inc(x_landed[t], 16)
            for e in EVENTS:
                if e[0] == "load":
                    u = e[1]
                    if u >= RAW:
                        sp.wait_ge(split_lo, u - RAW + 1)
                    sp.dma_start(raw[:, u % RAW, :], units[u]).then_inc(raw_landed[u % RAW], 16)
            sp.wait_ge(scaled, NT)
            sp.dma_start(gain[:], every_row(1)).then_inc(gain_landed, 16)
            with sp.Fori(0, FC // 2) as it:
                for b in range(4):
                    u = U_MLP + b + SPLIT - 1 + RAW
                    sp.wait_ge(split_lo, it * 4 + (u - RAW + 1))
                    sp.dma_start(raw[:, u % RAW, :], units[it * 4 + u]).then_inc(raw_landed[u % RAW], 16)
            sp.wait_ge(scaled, 2 * NT)
            sp.dma_start(gain[:], every_row(2)).then_inc(gain_landed, 16)
            for u in range(U_DOWN + SPLIT - 1 + RAW, N_UNITS):
                sp.wait_ge(split_lo, u - RAW + 1)
                sp.dma_start(raw[:, u % RAW, :], units[u]).then_inc(raw_landed[u % RAW], 16)
            for t in range(NT):
                sp.wait_ge(scaled, 2 * NT + t + 1)
                sp.dma_start(out[t * P:(t + 1) * P, :], xs[:, t, :]).then_inc(out_stored, 16)
            sp.wait_ge(out_stored, 16 * NT)

        @block.gpsimd
        def _(pool):
            pool.dma_start(hot, onehot).then_inc(table_landed, 16)
            pool.dma_start(rows, band_add[0:BIAS_HEADS, :]).then_inc(table_landed, 16)
            pool.dma_start(table[:], rel_bias).then_inc(table_landed, 16)
            pool.dma_start(fb[:], f_bias).then_inc(const_landed, 16)
            pool.dma_start(sink[:], sinks).then_inc(const_landed, 16)
            pool.dma_start(mix_g[:], mix_gain).then_inc(const_landed, 16)
            pool.dma_start(pick_f[:], pick).then_inc(const_landed, 16)
            pool.memset(ident[:], 0.0).then_inc(consts_ready, 1)
            pool.wait_ge(consts_ready, 1)
            pool.affine_select(out=ident[:], in_=ident[:], compare_op=ALU.not_equal, fill=1.0, base=0,
                               pattern=[[-1, P]], channel_multiplier=1).then_inc(consts_ready, 1)
            pool.memset(mirror[:], 0.0).then_inc(consts_ready, 1)
            pool.wait_ge(consts_ready, 3)
            pool.affine_select(out=mirror[:], in_=mirror[:], compare_op=ALU.not_equal, fill=1.0, base=1 - P,
                               pattern=[[1, P]], channel_multiplier=1).then_inc(consts_ready, 1)
            pool.memset(minus_half[:], -0.5).then_inc(consts_ready, 1)
            pool.memset(ones[:], 1.0).then_inc(consts_ready, 1)
            pool.memset(as_f32(decay[:]), 0.0).then_inc(consts_ready, 1)
            pool.memset(zero_row[:], 0.0).then_inc(consts_ready, 1)
            for buf in (pt_hi, pt_lo):
                pool.memset(as_f32(buf[:, :, 3 * PT_STRIDE + 2 * P:3 * PT_STRIDE + 3 * P]), 0.0).then_inc(consts_ready, 1)
            for e in EVENTS:
                if e[0] == "root":
                    _, which, t = e
                    pool.wait_ge(squared, NT * which + t + 1)
                    pool.tensor_scalar(mean[:, which, t:t + 1], ssq[:, which, t:t + 1], 1.0 / D_MODEL, EPS,
                                       ALU.mult, ALU.add).then_inc(mean_ready, 1)
                    pool.wait_ge(mean_ready, NT * which + t + 1)
                    pool.wait_ge(consts_ready, 5)
                    pool.tensor_tensor(rstd[:, which, t:t + 1], mean[:, which, t:t + 1], minus_half[:, 0:1],
                                       ALU.pow).then_inc(rstd_ready, 1)
                elif e[0] == "store_rows":
                    pool.wait_ge(bank_drained, 2)
                    pool.dma_start(bias_rows.ap(), rows).then_inc(rows_stored, 16)
                elif e[0] == "bias":
                    pair = e[1]
                    group, step = group_of(pair), 2 if group_of(pair) == GROUP_C else 1
                    if pair < 2:
                        pool.wait_ge(job_done, job_of["h", 0] + 1)
                    else:
                        pool.wait_ge(top_ready, 8 * (pair - 1))
                    if group == GROUP_D:
                        src = bass.AP(tensor=band_add.tensor, offset=MASK_ROW * ROW,
                                      ap=[[1, P], [0, 2], [1, SEQ]])
                    else:
                        pool.wait_ge(rows_stored, 16)
                        src = skewed(bias_rows, 4 * (group - 1) + head_of(pair, 0), step)
                    pool.dma_start(tb[:, pair % 2, :].rearrange("p (h c) -> p h c", h=2), src)\
                        .then_inc(bias_landed[pair % 2], 16)
                elif e[0] == "norm":
                    n = e[1]
                    width = keys_of(n)[4]
                    pool.wait_ge(inv_ready, n + 1)
                    pool.wait_ge(exp_ready, n + 1)
                    probs = s_buf[:, n % 3, 0:width]
                    pool.tensor_scalar(probs, probs, inv[:, n:n + 1], 1.0, ALU.mult, ALU.mult).then_inc(probs_ready, 1)
                elif e[0] == "values" and e[1] in (10, 11):
                    h = e[1]
                    pool.wait_ge(values_ready, h + 1)
                    for buf in (pt_hi, pt_lo):
                        pool.memset(as_f32(buf[:, h % 2, 2 * P:4 * P]), 0.0).then_inc(zeros_ready, 1)
                elif e[0] == "drain_stats":
                    g = e[1]
                    pool.wait_ge(bank_drained, e[2] + 1)
                    pool.tensor_tensor(g_rstd[:, g, :], g_mean[:, g, :], minus_half[:], ALU.pow).then_inc(g_rstd_ready, 1)
            for t in range(NT):
                pool.wait_ge(squared, 2 * NT + t + 1)
                pool.tensor_scalar(mean[:, 2, t:t + 1], ssq[:, 2, t:t + 1], 1.0 / D_MODEL, EPS,
                                   ALU.mult, ALU.add).then_inc(mean_ready, 1)
                pool.wait_ge(mean_ready, 2 * NT + t + 1)
                pool.tensor_tensor(rstd[:, 2, t:t + 1], mean[:, 2, t:t + 1], minus_half[:, 0:1],
                                   ALU.pow).then_inc(rstd_ready, 1)

        @block.scalar
        def _(act):
            def split(u):
                landed(act, u)
                if u >= SPLIT:
                    act.wait_ge(job_done, UNIT_JOB[u - SPLIT] + 1)
                act.activation(w_hi[:, u % SPLIT, :], raw[:, u % RAW, :], ACT.Copy).then_inc(split_hi, 1)

            def square(which, t, junk):
                act.activation(junk, xs[:, t, :], ACT.Square, accum_out=ssq[:, which, t:t + 1]).then_inc(squared, 1)

            for e in EVENTS:
                if e[0] == "split":
                    split(e[1])
                elif e[0] == "square":
                    _, which, t = e
                    if which == 0:
                        act.wait_ge(x_landed[t], 16)
                    else:
                        act.wait_ge(bank_drained, job_of["out", GROUP_C, 1, t] + 1)
                    square(which, t, ps[:, VALUE:VALUE + 2, :].rearrange("p a b -> p (a b)"))
                elif e[0] == "drain_h":
                    _, which, t, half, j = e
                    act.wait_ge(job_done, j + 1)
                    act.activation(h_hi[:, 4 * half:4 * half + 4, t * P:(t + 1) * P],
                                   ps[:, PROJ + j % 2, :].rearrange("p (k c) -> p k c", k=4), ACT.Copy).then_inc(job_hi, 1)
                elif e[0] == "drain" and e[1] in "qk":
                    _, kind, pair, j = e
                    act.wait_ge(job_done, j + 1)
                    if pair >= 2:
                        act.wait_ge(scores_ready, 8 * (pair - 1))
                    dst = q_hi[:, pair % 2, :] if kind == "q" else k_hi[:, kv_slot(pair), :]
                    act.activation(by_tiles(dst), projected(kind, j), ACT.Copy,
                                   scale=SCALE if kind == "q" else 1.0).then_inc(job_hi, 1)
                elif e[0] == "drain" and e[1] == "f":
                    act.wait_ge(decay_step, 2)
                    act.activation(s_buf[0:4, 1, :], s_buf[0:4, 1, :], ACT.Exp, scale=-1.0).then_inc(softplus_ready, 1)
                    act.wait_ge(softplus_ready, 1)
                    act.activation(s_buf[0:4, 1, :], s_buf[0:4, 1, :], ACT.Ln, bias=1.0).then_inc(softplus_ready, 1)
                elif e[0] == "drain_v":
                    _, pair, j = e
                    act.wait_ge(job_done, j + 1)
                    if pair >= 2:
                        act.wait_ge(values_ready, 2 * (pair - 1))
                    act.activation(v_hi[:, kv_slot(pair), :, :].rearrange("p a b -> p (a b)"), ps[:, PROJ + j % 2, :],
                                   ACT.Copy).then_inc(job_hi, 1)
                elif e[0] == "exp":
                    n = e[1]
                    pair, side, i, first, width = keys_of(n)
                    act.wait_ge(shift_ready, n + 1)
                    probs = s_buf[:, n % 3, 0:width]
                    act.activation(probs, probs, ACT.Exp, bias=shift[:, n:n + 1],
                                   accum_out=total[:, n:n + 1]).then_inc(exp_ready, 1)
                    if group_of(pair) == GROUP_C:
                        h = head_of(pair, side)
                        act.activation(sink_e[:, n:n + 1], sink[:, h:h + 1], ACT.Exp,
                                       bias=shift[:, n:n + 1]).then_inc(sink_ready, 1)
                elif e[0] == "keep":
                    n = e[1]
                    width = keys_of(n)[4]
                    act.wait_ge(turned, n + 1)
                    if n >= 8 and n % 4 == 0:
                        act.wait_ge(values_ready, n // 4 - 1)
                    act.activation(pt_blocks(pt_hi, n), ps[:, TURN + n % 2, 0:width].rearrange("p (j c) -> p j c", c=P),
                                   ACT.Copy).then_inc(kept_hi, 1)
                elif e[0] == "gather":
                    h = e[1]
                    pair, r = h // 2, HEAD_DIM * (h % 2)
                    act.wait_ge(values_ready, h + 1)
                    if pair >= MIX_SLOTS:
                        act.wait_ge(job_done, job_of["out", group_of(pair - MIX_SLOTS), 1, NT - 1] + 1)
                    head_out = ps[r:r + HEAD_DIM, VALUE + h % 2, :]
                    act.activation(mix_hi[r:r + HEAD_DIM, pair % MIX_SLOTS, :], head_out, ACT.Copy,
                                   scale=mix_g[r:r + HEAD_DIM, pair:pair + 1]).then_inc(gathered_hi, 1)
                    if h >= 4 and h % 4 == 0:
                        act.wait_ge(job_done, job_of["stats", h // 4 - 1] + 1)
                    act.activation(sq[r:r + HEAD_DIM, pair % 2, :], head_out, ACT.Square).then_inc(gathered_hi, 1)
            with act.Fori(0, FC // 2) as it:
                for b in range(2):
                    for part in range(2):
                        u = U_MLP + 2 * b + part + SPLIT - 1
                        act.wait_ge(raw_landed[u % RAW], it * 16 + 16 * (u // RAW + 1))
                        act.wait_ge(job_done, it * 4 + (JOBS + u - SPLIT - U_MLP + 1))
                        act.activation(w_hi[:, u % SPLIT, :], raw[:, u % RAW, :], ACT.Copy).then_inc(split_hi, 1)
                        if part == 0:
                            act.wait_ge(job_done, it * 4 + (JOBS + 2 * b + 1))
                            act.wait_ge(bank_drained, it * 2 + (JOBS + b - 1))
                            act.activation(act_g[:, b, :], ps[:, PROJ + b, :], ACT.Silu).then_inc(silu_ready, 1)
                    act.wait_ge(bank_drained, it * 2 + (JOBS + b + 1))
                    act.activation(gu_hi[:, it * 2 + b, :], gated[:, b, :], ACT.Copy).then_inc(gu_hi_ready, 1)
            for u in range(U_DOWN + SPLIT - 1, N_UNITS):
                landed(act, u)
                act.wait_ge(job_done, JOBS + u - SPLIT - U_MLP + 1)
                act.activation(w_hi[:, u % SPLIT, :], raw[:, u % RAW, :], ACT.Copy).then_inc(split_hi, 1)
            for t in range(NT):
                act.wait_ge(added, t + 1)
                square(2, t, ps[:, 2 * t:2 * t + 2, :].rearrange("p a b -> p (a b)"))

        @block.vector
        def _(dve):
            def split(u):
                dve.wait_ge(split_hi, u + 1)
                dve.tensor_tensor(w_lo[:, u % SPLIT, :], raw[:, u % RAW, :], as_f32(w_hi[:, u % SPLIT, :]),
                                  ALU.subtract).then_inc(split_lo, 1)

            def scale_rows(which, t, dst):
                dve.wait_ge(rstd_ready, NT * which + t + 1)
                dve.wait_ge(gain_landed, 16 * (which + 1))
                dve.scalar_tensor_tensor(dst, xs[:, t, :], rstd[:, which, t:t + 1], gain[:], ALU.mult,
                                         ALU.mult).then_inc(scaled, 1)

            decay_steps = [0]

            def step(ins):
                decay_steps[0] += 1
                ins.then_inc(decay_step, 1)
                dve.wait_ge(decay_step, decay_steps[0])

            for e in EVENTS:
                if e[0] == "split":
                    split(e[1])
                elif e[0] == "scale":
                    _, which, t = e
                    if t >= 2:
                        dve.wait_ge(job_done, job_at["h", which, t - 2] + 1)
                    scale_rows(which, t, tb[:, t % 2, :])
                elif e[0] == "drain_h":
                    _, which, t, half, j = e
                    dve.wait_ge(job_hi, hi_upto[j])
                    ks, ts = slice(4 * half, 4 * half + 4), slice(t * P, (t + 1) * P)
                    dve.tensor_tensor(h_lo[:, ks, ts], ps[:, PROJ + j % 2, :].rearrange("p (k c) -> p k c", k=4),
                                      as_f32(h_hi[:, ks, ts]), ALU.subtract).then_inc(bank_drained, 1)
                elif e[0] == "drain_table":
                    _, part, j = e
                    at, width = (0, SEQ) if part == 0 else (SEQ, ROW - SEQ)
                    dve.wait_ge(table_landed, 48)
                    dve.wait_ge(job_done, j + 1)
                    dve.tensor_tensor(rows[:, at:at + width], ps[0:BIAS_HEADS, PROJ + j % 2, 0:width],
                                      rows[:, at:at + width], ALU.add).then_inc(bank_drained, 1)
                elif e[0] == "drain" and e[1] in "qk":
                    _, kind, pair, j = e
                    hi, lo, slot = (q_hi, q_lo, pair % 2) if kind == "q" else (k_hi, k_lo, kv_slot(pair))
                    dve.wait_ge(job_hi, hi_upto[j])
                    dve.scalar_tensor_tensor(by_tiles(lo[:, slot, :]), projected(kind, j), SCALE if kind == "q" else 1.0,
                                             by_tiles(as_f32(hi[:, slot, :])), ALU.mult, ALU.subtract).then_inc(bank_drained, 1)
                elif e[0] == "drain" and e[1] == "v":
                    _, _, pair, j = e
                    if pair == 0:
                        dve.wait_ge(rows_stored, 16)
                    dve.wait_ge(job_done, j + 1)
                    dve.tensor_copy(vt[:, pair % 2, :], ps[:, PROJ + j % 2, :]).then_inc(bank_drained, 1)
                elif e[0] == "drain" and e[1] == "f":
                    j = e[3]
                    z, soft, log_f, c = (s_buf[0:4, k, :] for k in (0, 1, 2, 0))
                    dve.wait_ge(job_done, j + 1)
                    dve.wait_ge(const_landed, 64)
                    dve.tensor_scalar(z, ps[0:4, PROJ + j % 2, :], fb[:, 0:1], None, ALU.add).then_inc(bank_drained, 1)
                    dve.wait_ge(bank_drained, j + 1)
                    step(dve.tensor_copy(pick_r[:], pick_f[:]))
                    step(dve.scalar_tensor_tensor(soft, z, -1.0, z, ALU.mult, ALU.max))
                    dve.wait_ge(softplus_ready, 2)
                    step(dve.scalar_tensor_tensor(log_f, z, 0.0, soft, ALU.min, ALU.subtract))
                    dve.wait_ge(consts_ready, 10)
                    step(dve.tensor_tensor_scan(c, log_f, zero_row[:], 0.0, ALU.add, ALU.add))
                    step(dve.tensor_scalar(decay[0:4, :], c, -1.0, None, ALU.mult))
                    step(dve.tensor_scalar(decay[64:68, :], c, -1.0, None, ALU.mult))
                    for r in (32, 96):
                        step(dve.scalar_tensor_tensor(decay[r:r + 4, :], c, -1.0, as_f32(decay[0:4, :]), ALU.mult,
                                                      ALU.subtract))
                elif e[0] == "drain_v":
                    _, pair, j = e
                    slot = kv_slot(pair)
                    dve.wait_ge(job_hi, hi_upto[j])
                    dve.tensor_tensor(v_lo[:, slot, :, :].rearrange("p a b -> p (a b)"), ps[:, PROJ + j % 2, :],
                                      as_f32(v_hi[:, slot, :, :]).rearrange("p a b -> p (a b)"),
                                      ALU.subtract).then_inc(bank_drained, 1)
                elif e[0] == "max":
                    n = e[1]
                    pair, side, i, first, width = keys_of(n)
                    dve.wait_ge(scores_ready, n + 1)
                    if n % 8 == 0:
                        dve.wait_ge(bias_landed[pair % 2], 16 * (pair // 2 + 1))
                    if n >= 3:
                        dve.wait_ge(turned, n - 2)
                    least = sink[:, head_of(pair, side):head_of(pair, side) + 1] if group_of(pair) == GROUP_C else LOWEST
                    end = SEQ * (side + 1)
                    dve.tensor_tensor_reduce(s_buf[:, n % 3, 0:width], ps[:, SCORE + n % 2, 0:width],
                                             tb[:, pair % 2, end - width:end], 1.0, least, ALU.add, ALU.max,
                                             top[:, n:n + 1]).then_inc(top_ready, 1)
                    dve.wait_ge(top_ready, n + 1)
                    dve.tensor_scalar(shift[:, n:n + 1], top[:, n:n + 1], -1.0, None, ALU.mult).then_inc(shift_ready, 1)
                elif e[0] == "norm":
                    n = e[1]
                    dve.wait_ge(exp_ready, n + 1)
                    sums = total
                    if group_of(n // 8) == GROUP_C:
                        dve.wait_ge(sink_ready, n - 8 * 6 + 1)
                        dve.tensor_tensor(total2[:, n:n + 1], total[:, n:n + 1], sink_e[:, n:n + 1],
                                          ALU.add).then_inc(total_ready, 1)
                        dve.wait_ge(total_ready, n - 8 * 6 + 1)
                        sums = total2
                    dve.reciprocal(inv[:, n:n + 1], sums[:, n:n + 1]).then_inc(inv_ready, 1)
                elif e[0] == "keep":
                    n = e[1]
                    width = keys_of(n)[4]
                    dve.wait_ge(kept_hi, n + 1)
                    dve.tensor_tensor(pt_blocks(pt_lo, n), ps[:, TURN + n % 2, 0:width].rearrange("p (j c) -> p j c", c=P),
                                      as_f32(pt_blocks(pt_hi, n)), ALU.subtract).then_inc(kept_lo, 1)
                elif e[0] == "gather":
                    h = e[1]
                    pair, r = h // 2, HEAD_DIM * (h % 2)
                    dve.wait_ge(gathered_hi, 2 * (h + 1))
                    dve.scalar_tensor_tensor(mix_lo[r:r + HEAD_DIM, pair % MIX_SLOTS, :],
                                             ps[r:r + HEAD_DIM, VALUE + h % 2, :], mix_g[r:r + HEAD_DIM, pair:pair + 1],
                                             as_f32(mix_hi[r:r + HEAD_DIM, pair % MIX_SLOTS, :]), ALU.mult,
                                             ALU.subtract).then_inc(gathered_lo, 1)
                elif e[0] == "drain_stats":
                    _, g, j = e
                    dve.wait_ge(job_done, j + 1)
                    dve.tensor_scalar(g_mean[:, g, :], ps[:, PROJ + j % 2, :].rearrange("p (t c) -> p t c", c=P)[:, :, 0],
                                      1.0 / (4 * HEAD_DIM), EPS, ALU.mult, ALU.add).then_inc(bank_drained, 1)
                elif e[0] == "drain_out":
                    _, g, half, t, j = e
                    cols = slice(half * SEQ, (half + 1) * SEQ)
                    dve.wait_ge(job_done, j + 1)
                    dve.wait_ge(g_rstd_ready, g + 1)
                    dve.wait_ge(bank_drained, j)
                    dve.scalar_tensor_tensor(xs[:, t, cols], ps[:, PROJ + j % 2, :], g_rstd[:, g, t:t + 1],
                                             xs[:, t, cols], ALU.mult, ALU.add).then_inc(bank_drained, 1)
            with dve.Fori(0, FC // 2) as it:
                for b in range(2):
                    for part in range(2):
                        u = U_MLP + 2 * b + part + SPLIT - 1
                        dve.wait_ge(split_hi, it * 4 + (u + 1))
                        dve.tensor_tensor(w_lo[:, u % SPLIT, :], raw[:, u % RAW, :], as_f32(w_hi[:, u % SPLIT, :]),
                                          ALU.subtract).then_inc(split_lo, 1)
                    dve.wait_ge(silu_ready, it * 2 + (b + 1))
                    dve.wait_ge(job_done, it * 4 + (JOBS + 2 * b + 2))
                    dve.tensor_tensor(gated[:, b, :], ps[:, SCORE + b, :], act_g[:, b, :],
                                      ALU.mult).then_inc(bank_drained, 1)
                    dve.wait_ge(gu_hi_ready, it * 2 + (b + 1))
                    dve.tensor_tensor(gu_lo[:, it * 2 + b, :], gated[:, b, :], as_f32(gu_hi[:, it * 2 + b, :]),
                                      ALU.subtract).then_inc(gu_lo_ready, 1)
            for u in range(U_DOWN + SPLIT - 1, N_UNITS):
                split(u)

            def add_down(t):
                dve.wait_ge(down_done, t + 1)
                dve.tensor_tensor(xs[:, t, :], ps[:, 2 * t:2 * t + 2, :].rearrange("p a b -> p (a b)"), xs[:, t, :],
                                  ALU.add).then_inc(added, 1)

            for t in range(NT + 1):
                if t < NT:
                    add_down(t)
                if t >= 1:
                    scale_rows(2, t - 1, xs[:, t - 1, :])

        @block.tensor
        def _(pe):
            def thrice(bank, a, b, first, last):
                pe.matmul(bank, a[0], b[0], start=first, stop=False)
                pe.matmul(bank, a[0], b[1], start=False, stop=False)
                return pe.matmul(bank, a[1], b[0], start=False, stop=last)

            def bank_free(j):
                if j >= 2:
                    pe.wait_ge(bank_drained, j - 1)

            for e in EVENTS:
                if e[0] == "table":
                    _, part, j = e
                    at, width = (0, SEQ) if part == 0 else (SEQ, ROW - SEQ)
                    pe.wait_ge(table_landed, 48)
                    pe.matmul(ps[0:BIAS_HEADS, PROJ + j % 2, 0:width], table[:], hot[:, at:at + width], start=True,
                              stop=True).then_inc(job_done, 1)
                elif e[0] == "turn_h":
                    _, which, t, half, j = e
                    bank_free(j)
                    pe.wait_ge(consts_ready, 10)
                    pe.wait_ge(scaled, NT * which + t + 1)
                    for k in range(4):
                        at = (4 * half + k) * P
                        mm = pe.transpose(ps[:, PROJ + j % 2, k * P:(k + 1) * P], tb[:, t % 2, at:at + P], ident[:])
                    mm.then_inc(job_done, 1)
                elif e[0] == "piece":
                    _, kind, u, j, r = e
                    if r == 0:
                        bank_free(j)
                        pe.wait_ge(split_lo, u + 1)
                        if u == 0:
                            pe.wait_ge(bank_drained, job_at["h", 0, NT - 1] + 1)
                    for k in range((NK * r + 2) // 3, (NK * (r + 1) + 2) // 3):
                        cols = slice(k * P, (k + 1) * P)
                        mm = thrice(ps[:, PROJ + j % 2, :], (w_hi[:, u % SPLIT, cols], w_lo[:, u % SPLIT, cols]),
                                    (h_hi[:, k, :], h_lo[:, k, :]), k == 0, k == NK - 1)
                    if r == 2:
                        mm.then_inc(job_done, 1)
                elif e[0] == "turn_v":
                    _, pair, j = e
                    bank_free(j)
                    pe.wait_ge(bank_drained, job_of["v", pair] + 1)
                    for t in range(NT):
                        ts = slice(t * P, (t + 1) * P)
                        mm = pe.transpose(ps[:, PROJ + j % 2, ts], vt[:, pair % 2, ts], ident[:])
                    mm.then_inc(job_done, 1)
                elif e[0] == "scores":
                    n = e[1]
                    pair, side, i, first, width = keys_of(n)
                    r, qs = slice(HEAD_DIM * side, HEAD_DIM * side + HEAD_DIM), slice(i * P, (i + 1) * P)
                    ks = slice(first, first + max(width, 2 * P))
                    if n % 8 == 0:
                        pe.wait_ge(bank_drained, max(job_of["q", pair], job_of["k", pair]) + 1)
                    if n == 0:
                        pe.wait_ge(decay_step, 8)
                    if n >= 2:
                        pe.wait_ge(top_ready, n - 1)
                    bank, a, kv = ps[:, SCORE + n % 2, 0:ks.stop - ks.start], pair % 2, kv_slot(pair)
                    of_d = group_of(pair) == GROUP_D
                    mm = thrice(bank, (q_hi[r, a, qs], q_lo[r, a, qs]), (k_hi[r, kv, ks], k_lo[r, kv, ks]), True, not of_d)
                    if of_d:
                        mm = pe.matmul(bank, pick_r[r, head_of(pair, side), :], decay[r, ks], start=False, stop=True)
                    mm.then_inc(scores_ready, 1)
                elif e[0] == "turn":
                    n = e[1]
                    pe.wait_ge(probs_ready, n + 1)
                    if n >= 2:
                        pe.wait_ge(kept_lo, n - 1)
                    for k in range(keys_of(n)[4] // P):
                        ks = slice(k * P, (k + 1) * P)
                        mm = pe.transpose(ps[:, TURN + n % 2, ks], s_buf[:, n % 3, ks], mirror[:])
                    mm.then_inc(turned, 1)
                elif e[0] == "values":
                    h = e[1]
                    pair, slot = h // 2, kv_slot(h // 2)
                    banded = group_of(pair) == GROUP_C
                    pe.wait_ge(kept_lo, 4 * (h + 1))
                    if h % 2 == 0:
                        pe.wait_ge(bank_drained, job_of["v_turned", pair] + 1)
                    if h >= 2:
                        pe.wait_ge(gathered_lo, h - 1)
                    if banded and h < 14:
                        pe.wait_ge(zeros_ready, 2 * (h - 11))
                    for k in range(NT):
                        q0, q1 = (min(k, 2), NT if k == 0 or not banded else min(k + 2, NT))
                        moving = slice(PT_STRIDE * k + P * q0, PT_STRIDE * k + P * q1)
                        mm = thrice(ps[:, VALUE + h % 2, P * q0:P * q1], (v_hi[:, slot, k, :], v_lo[:, slot, k, :]),
                                    (pt_hi[:, h % 2, moving], pt_lo[:, h % 2, moving]), k == 0, k == NT - 1)
                    mm.then_inc(values_ready, 1)
                elif e[0] == "stats":
                    _, g, j = e
                    bank_free(j)
                    pe.wait_ge(gathered_hi, 8 * (g + 1))
                    for t in range(NT):
                        ts = slice(t * P, (t + 1) * P)
                        for c in range(2):
                            mm = pe.matmul(ps[:, PROJ + j % 2, ts], sq[:, c, ts], ones[:], start=c == 0, stop=c == 1)
                    mm.then_inc(job_done, 1)
                elif e[0] == "out":
                    _, g, half, t, u, j = e
                    bank_free(j)
                    if t == 0:
                        pe.wait_ge(split_lo, u + 1)
                        pe.wait_ge(gathered_lo, 4 * (g + 1))
                    ts = slice(t * P, (t + 1) * P)
                    for c in range(2):
                        slot, cols = (2 * g + c) % MIX_SLOTS, slice(c * SEQ, (c + 1) * SEQ)
                        mm = thrice(ps[:, PROJ + j % 2, :], (mix_hi[:, slot, ts], mix_lo[:, slot, ts]),
                                    (w_hi[:, u % SPLIT, cols], w_lo[:, u % SPLIT, cols]), c == 0, c == 1)
                    mm.then_inc(job_done, 1)
            pe.wait_ge(bank_drained, JOBS)
            pe.wait_ge(top_ready, STEPS)
            with pe.Fori(0, FC // 2) as it:
                for b in range(2):
                    for part in range(2):
                        u = U_MLP + 2 * b + part
                        pe.wait_ge(split_lo, it * 4 + (u + 1))
                        if part == 0:
                            pe.wait_ge(bank_drained, it * 2 + (JOBS + b - 1))
                        for k in range(NK):
                            cols = slice(k * P, (k + 1) * P)
                            mm = thrice(ps[:, 2 * part + b, :], (w_hi[:, u % SPLIT, cols], w_lo[:, u % SPLIT, cols]),
                                        (h_hi[:, k, :], h_lo[:, k, :]), k == 0, k == NK - 1)
                        mm.then_inc(job_done, 1)
            pe.wait_ge(bank_drained, JOBS + FC)
            for f in range(FC):
                u = U_DOWN + f
                pe.wait_ge(split_lo, u + 1)
                pe.wait_ge(gu_lo_ready, f + 1)
                for t in range(NT):
                    ts = slice(t * P, (t + 1) * P)
                    for half in range(2):
                        cols = slice(half * SEQ, (half + 1) * SEQ)
                        mm = thrice(ps[:, 2 * t + half, :], (gu_hi[:, f, ts], gu_lo[:, f, ts]),
                                    (w_hi[:, u % SPLIT, cols], w_lo[:, u % SPLIT, cols]), f == 0, f == FC - 1)
                    if f == FC - 1:
                        mm.then_inc(down_done, 1)
                if f < FC - 1:
                    mm.then_inc(job_done, 1)



def weight_units(w_in, w_out, w_gate, w_up, w_down):
    def tiles(w):
        w = np.pad(w, ((0, 0), (0, P - w.shape[1])))
        return w.reshape(NK, P, P).transpose(1, 0, 2).reshape(P, UNIT)

    def heads(pair):
        return [head_of(pair, side) for side in range(2)]

    def columns(start, picked):
        return np.concatenate([w_in[:, start + h * HEAD_DIM:start + (h + 1) * HEAD_DIM] for h in picked], axis=1)

    units = {}
    for e in plan()[0]:
        if e[0] == "piece" and e[4] == 0:
            units[e[2]] = (e[1],)
        if e[0] == "out" and e[3] == 0:
            _, g, half, _, u, _ = e
            rows = []
            for pair in (2 * g, 2 * g + 1):
                at = [MIX_AT[g] + h * HEAD_DIM for h in heads(pair)]
                rows.append(np.concatenate([w_out[a:a + HEAD_DIM, half * SEQ:(half + 1) * SEQ] for a in at]))
            units[u] = np.concatenate(rows, axis=1)
    pending = [u for u in sorted(units) if isinstance(units[u], tuple)]
    seen = {"q": 0, "k": 0, "v": 0}
    for u in pending:
        kind = units[u][0]
        if kind == "f":
            units[u] = tiles(w_in[:, F_AT:F_AT + 4])
            continue
        pair = seen[kind]
        seen[kind] += 1
        g = group_of(pair)
        if kind == "q":
            units[u] = tiles(columns(Q_AT[g], heads(pair)))
        else:
            picked = [0, 1] if g == GROUP_C else heads(pair)
            units[u] = tiles(columns((K_AT if kind == "k" else V_AT)[g], picked))
    out = [units[u] for u in range(len(units))]
    for f in range(FC):
        out += [tiles(w_gate[:, f * P:(f + 1) * P]), tiles(w_up[:, f * P:(f + 1) * P])]
    out += [w_down[f * P:(f + 1) * P, :] for f in range(FC)]
    return np.stack(out)


def kernel(x, norm1_g, w_in, f_bias, sinks, mix_norm_g, w_out, norm2_g, w_gate, w_up, w_down, rel_bias, final_g):
    import concourse.bacc as bacc
    from concourse.bass_utils import run_bass_kernel_spmd

    arrays = [np.asarray(a) for a in (x, norm1_g, w_in, f_bias, sinks, mix_norm_g, w_out, norm2_g, w_gate, w_up,
                                      w_down, rel_bias, final_g)]
    x, norm1_g, w_in, f_bias, sinks, mix_norm_g, w_out, norm2_g, w_gate, w_up, w_down, rel_bias, final_g = arrays
    onehot, band_add, pick = band_constants()
    mix_gain = np.stack([np.concatenate([mix_norm_g[0, MIX_AT[group_of(p)] + h * HEAD_DIM:][:HEAD_DIM]
                                         for h in (head_of(p, 0), head_of(p, 1))]) for p in range(PAIRS)], axis=1)
    ins = {
        "x": x[0],
        "units": weight_units(w_in[0], w_out[0], w_gate[0], w_up[0], w_down[0]),
        "gains": np.stack([norm1_g[0], norm2_g[0], final_g]),
        "mix_gain": mix_gain,
        "f_bias": f_bias.reshape(4, 1),
        "sinks": np.broadcast_to(sinks, (P, 4)),
        "rel_bias": rel_bias,
        "onehot": onehot,
        "band_add": band_add,
        "pick": pick,
    }
    ins = {f"in_{name}": np.ascontiguousarray(a) for name, a in ins.items()}
    nc = bacc.Bacc("TRN2", target_bir_lowering=False, num_devices=1)
    args = [nc.dram_tensor(name, a.shape, mybir.dt.from_np(a.dtype), kind="ExternalInput").ap() for name, a in ins.items()]
    out = nc.dram_tensor("out", (SEQ, D_MODEL), F32, kind="ExternalOutput").ap()
    hybrid_layer(nc, *args, out)
    r = run_bass_kernel_spmd(nc, [ins], core_ids=[0])
    return np.asarray(r.results[0]["out"]).reshape(1, SEQ, D_MODEL)
```

```python
from contextlib import ExitStack

import numpy as np
import concourse.bass as bass
from concourse import mybir

F32 = mybir.dt.float32
F32R = mybir.dt.float32r
ALU = mybir.AluOpType
ACT = mybir.ActivationFunctionType

P = 128
SEQ = 512
D_MODEL = 1024
HEAD_DIM = 64
N_BUCKETS = 32
T5_MAX_DISTANCE = 2048
D_FF = 2816
EPS = 1e-6
NEG = -1e30
SCALE = HEAD_DIM ** -0.5
LOWEST = -3.0e38

NT = SEQ // P
NK = D_MODEL // P
FC = D_FF // P
PAIRS = 8
STEPS = 8 * PAIRS
GROUP_D, GROUP_A, GROUP_B, GROUP_C = range(4)
RAW = 4
SPLIT = 4
UNIT = NK * P
MIX_SLOTS = 6
MIX_AT = [768, 0, 256, 512]
Q_AT = [2048, 0, 768, 1536]
K_AT = [2304, 256, 1024, 1792]
V_AT = [2560, 512, 1280, 1920]
F_AT = 2816
ROW = 640
BIAS_HEADS = 12
MASK_ROW = BIAS_HEADS
PIECES = [10, 10, 10, 10, 15, 14, 12, 8]
WARM_UP = 20
LEAD = 3
PT_STRIDE = 384
PT_WIDTH = 3 * PT_STRIDE + SEQ


def group_of(pair):
    return pair // 2


def head_of(pair, side):
    c = pair % 2
    return c + 2 * side if group_of(pair) == GROUP_C else 2 * c + side


def keys_of(n):
    pair, side, i = n // 8, n // 4 % 2, n % 4
    first = P * (i - 1) if group_of(pair) == GROUP_C and i else 0
    return pair, side, i, first, P * (i + 1) - first


def kv_slot(pair):
    return pair % 2 if pair < 7 else 0


def plan():
    events, unit_job, count = [], {}, {"job": 0, "unit": 0}
    emitted = {"scores": 0, "values": 0}

    def job():
        count["job"] += 1
        return count["job"] - 1

    def next_unit():
        u = count["unit"]
        count["unit"] += 1
        return u

    def ahead(u):
        events.append(("split", u + SPLIT - 1))
        events.append(("load", u + SPLIT - 1 + RAW))

    def projection(kind, pair):
        u, j = next_unit(), job()
        unit_job[u] = j
        for r in range(3):
            ks = range((NK * r + 2) // 3, (NK * (r + 1) + 2) // 3)
            events.append(("piece", kind, u, j, ks, slice(0, SEQ)))
            if r == 1:
                ahead(u)
            yield
        while kind in "qk" and emitted["scores"] < 8 * (pair - 1):
            yield
        events.append(("drain", kind, pair, j))

    def turn_values(pair):
        j = job()
        events.append(("turn_v", pair, j))
        yield
        while emitted["values"] < 2 * (pair - 1):
            yield
        events.append(("drain_v", pair, j))

    def projections(pair):
        if pair == 7:
            return projection("q", pair)
        return chain(projection("v", pair), projection("q", pair), turn_values(pair), projection("k", pair))

    def output(group, half):
        u = next_unit()
        for t in range(NT):
            j = job()
            unit_job[u] = j
            events.append(("out", group, half, t, u, j))
            if t == 1:
                ahead(u)
            yield
            events.append(("drain_out", group, half, t, j))

    def chain(*parts):
        for part in parts:
            yield from part

    def run(filler):
        for _ in filler:
            pass

    def normed(which, *stages):
        for stage, t in stages:
            events.append((stage, which, t))

    for u in range(RAW):
        events.append(("load", u))
    tables = [(part, job()) for part in range(2)]
    f_u, f_j, v_u, v_j = next_unit(), job(), next_unit(), job()
    unit_job[f_u], unit_job[v_u] = f_j, v_j

    def half_product(kind, u, j, half):
        events.append(("piece", kind, u, j, range(NK), slice(half * SEQ // 2, (half + 1) * SEQ // 2)))

    def split_and_load(u):
        events.append(("split", u))
        events.append(("load", u + RAW))

    normed(0, ("square", 0), ("root", 0), ("square", 1), ("root", 1), ("scale", 0), ("turn_h", 0), ("scale", 1),
           ("square", 2), ("root", 2), ("drain_h", 0), ("turn_h", 1), ("scale", 2), ("square", 3), ("root", 3),
           ("drain_h", 1))
    split_and_load(0)
    for part, j in tables:
        events.append(("table", part, j))
        events.append(("drain_table", part, j))
    normed(0, ("turn_h", 2), ("scale", 3), ("drain_h", 2))
    half_product("f", f_u, f_j, 0)
    split_and_load(1)
    normed(0, ("turn_h", 3), ("drain_h", 3))
    events.append(("store_rows",))
    half_product("v", v_u, v_j, 0)
    split_and_load(2)
    half_product("f", f_u, f_j, 1)
    half_product("v", v_u, v_j, 1)
    events.append(("drain", "f", 0, f_j))
    stages = list(range(4))
    ahead(f_u)
    ahead(v_u)
    events.append(("drain", "v", 0, v_j))
    events.append(("bias", 0))
    events.append(("bias", 1))
    for _ in chain(projection("q", 0), turn_values(0), projection("k", 0)):
        if stages:
            events.append(("decays", stages.pop(0)))

    fillers = [projections(pair + 1) for pair in range(PAIRS - 1)] + [chain()]
    fillers[4] = chain(fillers[4], output(GROUP_D, 0))
    fillers[5] = chain(fillers[5], output(GROUP_D, 1))
    fillers[6] = chain(fillers[6], output(GROUP_A, 0), output(GROUP_A, 1))
    fillers[7] = chain(output(GROUP_B, 0), output(GROUP_B, 1))

    def fill(slot):
        pair, at = slot // 16, slot % 16
        if pair >= PAIRS:
            next(fillers[-1], None)
            return
        share = PIECES[pair] / 16
        for _ in range(int(share * (at + 1) + 1e-6) - int(share * at + 1e-6)):
            next(fillers[pair], None)
        if at == 15 and pair < PAIRS - 1:
            run(fillers[pair])

    for slot in range(LEAD):
        fill(slot)
    for s in range(STEPS + 5):
        if s < STEPS:
            events.append(("scores", s))
            emitted["scores"] += 1
        fill(2 * s + LEAD)
        if s < STEPS:
            events.append(("max", s))
            events.append(("exp", s))
        if 0 <= s - 1 < STEPS:
            events.append(("norm", s - 1))
        if 0 <= s - 2 < STEPS:
            events.append(("turn", s - 2))
            events.append(("keep", s - 2))
        fill(2 * s + 1 + LEAD)
        if s >= 6 and (s - 6) % 4 == 0 and (s - 6) // 4 < 2 * PAIRS:
            events.append(("values", (s - 6) // 4))
            emitted["values"] += 1
        if s >= 7 and (s - 7) % 4 == 0:
            events.append(("gather", (s - 7) // 4))
        if s % 8 == 2 and 2 <= s // 8 + 1 < PAIRS:
            events.append(("bias", s // 8 + 1))
        if s % 16 == 4 and s > 16 and s < STEPS:
            events.append(("stats", s // 16 - 1))
        if s == STEPS // 2:
            events.append(("gain", 1))
    run(fillers[-1])

    events.append(("stats", GROUP_C))
    c_units = next_unit(), next_unit()

    def out_tile(t):
        jobs = job(), job()
        for half in range(2):
            unit_job[c_units[half]] = jobs[half]
            events.append(("out", GROUP_C, half, t, c_units[half], jobs[half]))
        for half in range(2):
            events.append(("drain_out", GROUP_C, half, t, jobs[half]))

    out_tile(0)
    ahead(c_units[0])
    normed(1, ("square", 0), ("root", 0))
    out_tile(1)
    normed(1, ("scale", 0), ("square", 1), ("root", 1))
    out_tile(2)
    normed(1, ("turn_h", 0), ("scale", 1), ("drain_h", 0), ("square", 2), ("root", 2))
    out_tile(3)
    normed(1, ("turn_h", 1), ("scale", 2), ("drain_h", 1), ("square", 3), ("root", 3), ("turn_h", 2), ("scale", 3),
           ("drain_h", 2))
    events.append(("mlp", 0, 0))
    normed(1, ("turn_h", 3))
    normed(1, ("drain_h", 3))
    ahead(c_units[1])
    events.append(("mlp", 1, 0))
    events.append(("mlp", 0, 1))
    events.append(("mlp", 1, 1))
    return events, unit_job, count["job"], count["unit"]


def band_constants():
    dist = SEQ - 1 - np.arange(ROW)
    n = np.maximum(dist, 0)
    exact = N_BUCKETS // 2
    large = exact + (np.log(np.maximum(n, 1) / exact) / np.log(T5_MAX_DISTANCE / exact)
                     * (N_BUCKETS - exact)).astype(np.int64)
    bucket = np.where(n < exact, n, np.minimum(large, N_BUCKETS - 1))
    onehot = (np.arange(N_BUCKETS)[:, None] == bucket).astype(np.float32)
    causal = dist >= 0
    bands = (dist <= 128).astype(int) + (dist % 4 == 0) + (dist % 16 == 0)
    add = np.zeros((BIAS_HEADS + 1, ROW), np.float32)
    add[0:4] = np.where(causal & (bands > 0), np.log(np.maximum(bands, 1)), NEG)
    add[4:8] = np.where(causal, 0.0, NEG)
    add[8:12] = np.where(causal & (dist < 128), 0.0, NEG)
    add[MASK_ROW] = np.where(causal, 0.0, NEG)
    pick = np.zeros((P, 4, P), np.float32)
    for h in range(4):
        pick[h::32, h] = 1.0
    return onehot, add, pick


def hybrid_layer(nc, x, units, gains, mix_gain, f_bias, sinks, rel_bias, onehot, band_add, pick, out):
    EVENTS, UNIT_JOB, JOBS, U_MLP = plan()
    U_DOWN = U_MLP + 2 * FC
    N_UNITS = U_DOWN + FC
    HEADS = 2 * PAIRS
    hi_upto, job_of, hi_count = {}, {}, 0
    for e in EVENTS:
        if e[0] == "drain_v" or (e[0] == "drain" and e[1] in "qk"):
            hi_count += 1
            hi_upto[e[-1]] = hi_count
        if e[0] == "drain":
            job_of[e[1], e[2]] = e[3]
        if e[0] == "drain_v":
            job_of["v_turned", e[1]] = e[2]
        if e[0] == "out":
            job_of["out", e[1], e[2], e[3]] = e[5]
    for what in ("k", "v", "v_turned"):
        job_of[what, 7] = job_of[what, 6]

    bias_rows = nc.dram_tensor("bias_rows", (BIAS_HEADS, ROW), F32, kind="Internal")

    def skewed(rows, row, step):
        return bass.AP(tensor=rows, offset=row * ROW, ap=[[1, P], [step * ROW, 2], [1, SEQ]])

    with ExitStack() as ctx:
        def sb(name, shape, dt=F32, stack=ctx):
            return stack.enter_context(nc.sbuf_tensor(name, shape, dt))

        def sem(name):
            return ctx.enter_context(nc.semaphore(name))

        xs = sb("xs", [P, NT, D_MODEL])
        h_hi = sb("h_hi", [P, NK, SEQ], F32R)
        h_lo = sb("h_lo", [P, NK, SEQ], F32R)
        raw = sb("raw", [P, RAW, UNIT])
        w_hi = sb("w_hi", [P, SPLIT, UNIT], F32R)
        w_lo = sb("w_lo", [P, SPLIT, UNIT], F32R)
        gain = sb("gain", [P, D_MODEL])
        ident = sb("ident", [P, P])
        mirror = sb("mirror", [P, P])
        ones = sb("ones", [P, P])
        table = sb("table", [N_BUCKETS, BIAS_HEADS])
        mix_g = sb("mix_g", [P, PAIRS])
        fb = sb("fb", [4, 1])
        sink = sb("sink", [P, 4])
        minus_half = sb("minus_half", [P, NT])
        zero_row = sb("zero_row", [4, SEQ])
        ssq = sb("ssq", [P, 3, NT])
        mean = sb("mean", [P, 3, NT])
        rstd = sb("rstd", [P, 3, NT])
        ssq_out = sb("ssq_out", [P, NT, 2])
        part_mean = sb("part_mean", [P, NT])
        g_mean = sb("g_mean", [P, 4, NT])
        g_rstd = sb("g_rstd", [P, 4, NT])
        top = sb("top", [P, STEPS])
        shift = sb("shift", [P, STEPS])
        total = sb("total", [P, STEPS])
        sink_e = sb("sink_e", [P, STEPS])
        total2 = sb("total2", [P, STEPS])
        inv = sb("inv", [P, STEPS])
        tb = sb("tb", [P, 2, 1024])
        attn = ctx.enter_context(ExitStack())
        q_hi = sb("q_hi", [P, 2, SEQ], F32R, attn)
        q_lo = sb("q_lo", [P, 2, SEQ], F32R, attn)
        k_hi = sb("k_hi", [P, 2, SEQ], F32R, attn)
        k_lo = sb("k_lo", [P, 2, SEQ], F32R, attn)
        v_hi = sb("v_hi", [P, 2, NT, P], F32R, attn)
        v_lo = sb("v_lo", [P, 2, NT, P], F32R, attn)
        pt_hi = sb("pt_hi", [P, 2, PT_WIDTH], F32R, attn)
        pt_lo = sb("pt_lo", [P, 2, PT_WIDTH], F32R, attn)
        mix_hi = sb("mix_hi", [P, MIX_SLOTS, SEQ], F32R, attn)
        mix_lo = sb("mix_lo", [P, MIX_SLOTS, SEQ], F32R, attn)
        decay = sb("decay", [P, SEQ], F32R, attn)
        pick_r = sb("pick_r", [P, 4, P], F32R, attn)
        pick_f = sb("pick_f", [P, 4, P], F32, attn)
        s_buf = sb("s_buf", [P, 3, SEQ], F32, attn)
        sq = sb("sq", [P, 2, SEQ], F32, attn)
        vt = sb("vt", [P, 2, SEQ], F32, attn)
        attn.close()
        mlp = ctx.enter_context(ExitStack())
        gu_hi = sb("gu_hi", [P, FC, SEQ], F32R, mlp)
        gu_lo = sb("gu_lo", [P, FC, SEQ], F32R, mlp)
        act_g, gated = tb[:, :, 0:SEQ], tb[:, :, SEQ:2 * SEQ]
        hot = sq[0:N_BUCKETS, :, :].rearrange("p a b -> p (a b)")[:, 0:ROW]
        rows = vt[0:BIAS_HEADS, :, :].rearrange("p a b -> p (a b)")[:, 0:ROW]

        ps = ctx.enter_context(nc.psum_tensor("ps", [P, 8, SEQ], F32))
        PROJ, SCORE, TURN, VALUE = 0, 2, 4, 6

        x_landed = [sem(f"x_landed{t}") for t in range(NT)]
        gain_landed = sem("gain_landed")
        const_landed = sem("const_landed")
        table_landed = sem("table_landed")
        rows_stored = sem("rows_stored")
        bias_landed = [sem(f"bias_landed{i}") for i in range(2)]
        raw_landed = [sem(f"raw_landed{i}") for i in range(RAW)]
        out_stored = sem("out_stored")
        consts_ready = sem("consts_ready")
        squared = sem("squared")
        mean_ready = sem("mean_ready")
        rstd_ready = sem("rstd_ready")
        scaled = sem("scaled")
        rows_turned = sem("rows_turned")
        rows_hi = sem("rows_hi")
        rows_kept = sem("rows_kept")
        job_done = sem("job_done")
        job_hi = sem("job_hi")
        bank_drained = sem("bank_drained")
        split_hi = sem("split_hi")
        split_lo = sem("split_lo")
        decay_step = sem("decay_step")
        softplus_ready = sem("softplus_ready")
        scores_ready = sem("scores_ready")
        top_ready = sem("top_ready")
        shift_ready = sem("shift_ready")
        exp_ready = sem("exp_ready")
        sink_ready = sem("sink_ready")
        total_ready = sem("total_ready")
        inv_ready = sem("inv_ready")
        probs_ready = sem("probs_ready")
        turned = sem("turned")
        kept_hi = sem("kept_hi")
        kept_lo = sem("kept_lo")
        values_ready = sem("values_ready")
        gathered_hi = sem("gathered_hi")
        gathered_lo = sem("gathered_lo")
        zeros_ready = sem("zeros_ready")
        squares_added = sem("squares_added")
        stats_done = sem("stats_done")
        g_mean_ready = sem("g_mean_ready")
        g_rstd_ready = sem("g_rstd_ready")
        silu_ready = sem("silu_ready")
        gu_hi_ready = sem("gu_hi_ready")
        gu_lo_ready = sem("gu_lo_ready")
        down_done = sem("down_done")
        added = sem("added")

        def as_f32(ap):
            return ap.bitcast(F32)

        def landed(eng, u):
            eng.wait_ge(raw_landed[u % RAW], 16 * (u // RAW + 1))

        def pt_blocks(buf, n):
            _, _, i, first, width = keys_of(n)
            j0, nj = first // P, width // P
            at = P * i + PT_STRIDE * j0
            slot = buf[:, n // 4 % 2, :]
            return bass.AP(tensor=slot.tensor, offset=slot.offset + at, ap=[list(slot.ap[0]), [PT_STRIDE, nj], [1, P]])

        def projected(kind, j):
            bank = ps[:, PROJ + j % 2, :]
            if kind == "q":
                return bass.AP(tensor=bank.tensor, offset=bank.offset + P - 1, ap=[list(bank.ap[0]), [P, NT], [-1, P]])
            return bank.rearrange("p (t c) -> p t c", c=P)

        def by_tiles(ap):
            return ap.rearrange("p (t c) -> p t c", c=P)

        def every_row(which):
            return bass.AP(tensor=gains.tensor, offset=which * D_MODEL, ap=[[0, P], [1, D_MODEL]])

        block = ctx.enter_context(nc.Block())

        @block.sync
        def _(sp):
            sp.dma_start(xs[:, 0, :], x[0:P, :]).then_inc(x_landed[0], 16)
            for t in range(1, NT):
                sp.dma_start(xs[:, t, :], x[t * P:(t + 1) * P, :]).then_inc(x_landed[t], 16)
            sp.dma_start(hot, onehot).then_inc(table_landed, 16)
            sp.dma_start(rows, band_add[0:BIAS_HEADS, :]).then_inc(table_landed, 16)
            sp.dma_start(table[:], rel_bias).then_inc(table_landed, 16)
            for e in EVENTS:
                if e[0] == "load":
                    u = e[1]
                    if u == RAW:
                        sp.dma_start(fb[:], f_bias).then_inc(const_landed, 16)
                        sp.dma_start(sink[:], sinks).then_inc(const_landed, 16)
                        sp.dma_start(mix_g[:], mix_gain).then_inc(const_landed, 16)
                        sp.dma_start(pick_f[:], pick).then_inc(const_landed, 16)
                    if u >= RAW:
                        sp.wait_ge(split_lo, u - RAW + 1)
                    sp.dma_start(raw[:, u % RAW, :], units[u]).then_inc(raw_landed[u % RAW], 16)
                elif e[0] == "store_rows":
                    sp.wait_ge(bank_drained, 2)
                    sp.dma_start(bias_rows.ap(), rows).then_inc(rows_stored, 16)
                elif e[0] == "bias":
                    pair = e[1]
                    group, step = group_of(pair), 2 if group_of(pair) == GROUP_C else 1
                    if pair < 2:
                        sp.wait_ge(rows_turned, 2 * NT)
                    else:
                        sp.wait_ge(top_ready, 8 * (pair - 1))
                    if group == GROUP_D:
                        src = bass.AP(tensor=band_add.tensor, offset=MASK_ROW * ROW,
                                      ap=[[1, P], [0, 2], [1, SEQ]])
                    else:
                        sp.wait_ge(rows_stored, 16)
                        src = skewed(bias_rows, 4 * (group - 1) + head_of(pair, 0), step)
                    sp.dma_start(tb[:, pair % 2, :].rearrange("p (h c) -> p h c", h=2), src)\
                        .then_inc(bias_landed[pair % 2], 16)
                elif e[0] == "gain":
                    sp.wait_ge(scaled, NT)
                    sp.dma_start(gain[:], every_row(1)).then_inc(gain_landed, 16)
            with sp.Fori(0, FC // 2) as it:
                for b in range(4):
                    u = U_MLP + b + SPLIT - 1 + RAW
                    sp.wait_ge(split_lo, it * 4 + (u - RAW + 1))
                    sp.dma_start(raw[:, u % RAW, :], units[it * 4 + u]).then_inc(raw_landed[u % RAW], 16)
            sp.wait_ge(scaled, 2 * NT)
            sp.dma_start(gain[:], every_row(2)).then_inc(gain_landed, 16)
            for u in range(U_DOWN + SPLIT - 1 + RAW, N_UNITS):
                sp.wait_ge(split_lo, u - RAW + 1)
                sp.dma_start(raw[:, u % RAW, :], units[u]).then_inc(raw_landed[u % RAW], 16)
            for m in range(2 * NT):
                sp.wait_ge(scaled, 2 * NT + m + 1)
                at = (m // 2, slice(m % 2 * SEQ, (m % 2 + 1) * SEQ))
                sp.dma_start(out[at[0] * P:(at[0] + 1) * P, at[1]], xs[:, at[0], at[1]]).then_inc(out_stored, 16)
            sp.wait_ge(out_stored, 16 * 2 * NT)

        @block.gpsimd
        def _(pool):
            pool.memset(ones[:], 1.0).then_inc(consts_ready, 1)
            pool.memset(ident[:], 0.0).then_inc(consts_ready, 1)
            pool.wait_ge(consts_ready, 2)
            pool.affine_select(out=ident[:], in_=ident[:], compare_op=ALU.not_equal, fill=1.0, base=0,
                               pattern=[[-1, P]], channel_multiplier=1).then_inc(consts_ready, 1)
            pool.memset(mirror[:], 0.0).then_inc(consts_ready, 1)
            pool.wait_ge(consts_ready, 4)
            pool.affine_select(out=mirror[:], in_=mirror[:], compare_op=ALU.not_equal, fill=1.0, base=1 - P,
                               pattern=[[1, P]], channel_multiplier=1).then_inc(consts_ready, 1)
            pool.memset(minus_half[:], -0.5).then_inc(consts_ready, 1)
            pool.memset(as_f32(decay[:]), 0.0).then_inc(consts_ready, 1)
            pool.memset(zero_row[:], 0.0).then_inc(consts_ready, 1)
            for buf in (pt_hi, pt_lo):
                pool.memset(as_f32(buf[:, :, 3 * PT_STRIDE + 2 * P:3 * PT_STRIDE + 3 * P]), 0.0).then_inc(consts_ready, 1)
            for e in EVENTS:
                if e[0] == "root":
                    _, which, t = e
                    pool.wait_ge(squared, NT * which + t + 1)
                    pool.tensor_scalar(mean[:, which, t:t + 1], ssq[:, which, t:t + 1], 1.0 / D_MODEL, EPS,
                                       ALU.mult, ALU.add).then_inc(mean_ready, 1)
                    pool.wait_ge(mean_ready, NT * which + t + 1)
                    pool.wait_ge(consts_ready, 6)
                    pool.tensor_tensor(rstd[:, which, t:t + 1], mean[:, which, t:t + 1], minus_half[:, 0:1],
                                       ALU.pow).then_inc(rstd_ready, 1)
                elif e[0] == "norm":
                    n = e[1]
                    width = keys_of(n)[4]
                    pool.wait_ge(inv_ready, n + 1)
                    pool.wait_ge(exp_ready, n + 1)
                    probs = s_buf[:, n % 3, 0:width]
                    pool.tensor_scalar(probs, probs, inv[:, n:n + 1], 1.0, ALU.mult, ALU.mult).then_inc(probs_ready, 1)
                elif e[0] == "values" and e[1] in (10, 11):
                    h = e[1]
                    pool.wait_ge(values_ready, h + 1)
                    for buf in (pt_hi, pt_lo):
                        pool.memset(as_f32(buf[:, h % 2, 2 * P:4 * P]), 0.0).then_inc(zeros_ready, 1)
                elif e[0] == "stats":
                    g = e[1]
                    pool.wait_ge(gathered_hi, 8 * (g + 1))
                    pool.tensor_tensor(sq[:, 0, :], sq[:, 0, :], sq[:, 1, :], ALU.add).then_inc(squares_added, 1)
                    pool.wait_ge(g_mean_ready, g + 1)
                    pool.tensor_tensor(g_rstd[:, g, :], g_mean[:, g, :], minus_half[:], ALU.pow).then_inc(g_rstd_ready, 1)
            for t in range(NT):
                pool.wait_ge(squared, 2 * NT + 2 * t + 1)
                pool.tensor_scalar(part_mean[:, t:t + 1], ssq_out[:, t, 0:1], 1.0 / D_MODEL, EPS,
                                   ALU.mult, ALU.add).then_inc(mean_ready, 1)
                pool.wait_ge(squared, 2 * NT + 2 * t + 2)
                pool.wait_ge(mean_ready, 2 * NT + 2 * t + 1)
                pool.tensor_scalar(mean[:, 2, t:t + 1], ssq_out[:, t, 1:2], 1.0 / D_MODEL, part_mean[:, t:t + 1],
                                   ALU.mult, ALU.add).then_inc(mean_ready, 1)
                pool.wait_ge(mean_ready, 2 * NT + 2 * t + 2)
                pool.tensor_tensor(rstd[:, 2, t:t + 1], mean[:, 2, t:t + 1], minus_half[:, 0:1],
                                   ALU.pow).then_inc(rstd_ready, 1)

        @block.scalar
        def _(act):
            act.dma_start(gain[:], every_row(0)).then_inc(gain_landed, 16)

            def split(u):
                landed(act, u)
                if u >= SPLIT:
                    act.wait_ge(job_done, UNIT_JOB[u - SPLIT] + 1)
                act.activation(w_hi[:, u % SPLIT, :], raw[:, u % RAW, :], ACT.Copy).then_inc(split_hi, 1)

            for e in EVENTS:
                if e[0] == "split":
                    split(e[1])
                elif e[0] == "square":
                    _, which, t = e
                    if which == 0:
                        act.wait_ge(x_landed[t], 16)
                    else:
                        act.wait_ge(bank_drained, job_of["out", GROUP_C, 1, t] + 1)
                    if NT * which + t >= 1:
                        act.wait_ge(squared, NT * which + t)
                    act.activation(ps[:, VALUE:VALUE + 2, :].rearrange("p a b -> p (a b)"), xs[:, t, :], ACT.Square,
                                   accum_out=ssq[:, which, t:t + 1]).then_inc(squared, 1)
                elif e[0] == "drain_h":
                    _, which, t = e
                    for half in range(2):
                        act.wait_ge(rows_turned, 2 * (NT * which + t) + half + 1)
                        if which == 1 and t == 0 and half == 0:
                            act.wait_ge(job_done, job_of["q", PAIRS - 1] + 1)
                        act.activation(h_hi[:, 4 * half:4 * half + 4, t * P:(t + 1) * P],
                                       ps[:, TURN + half, :].rearrange("p (k c) -> p k c", k=4),
                                       ACT.Copy).then_inc(rows_hi, 1)
                elif e[0] == "drain" and e[1] in "qk":
                    _, kind, pair, j = e
                    act.wait_ge(job_done, j + 1)
                    if pair >= 2:
                        act.wait_ge(scores_ready, 8 * (pair - 1))
                    dst = q_hi[:, pair % 2, :] if kind == "q" else k_hi[:, kv_slot(pair), :]
                    act.activation(by_tiles(dst), projected(kind, j), ACT.Copy,
                                   scale=SCALE if kind == "q" else 1.0).then_inc(job_hi, 1)
                elif e[0] == "decays" and e[1] == 0:
                    act.wait_ge(decay_step, 1)
                    act.activation(s_buf[0:4, 1, :], s_buf[0:4, 1, :], ACT.Exp, scale=-1.0).then_inc(softplus_ready, 1)
                    act.wait_ge(softplus_ready, 1)
                    act.activation(s_buf[0:4, 1, :], s_buf[0:4, 1, :], ACT.Ln, bias=1.0).then_inc(softplus_ready, 1)
                elif e[0] == "drain_v":
                    _, pair, j = e
                    act.wait_ge(job_done, j + 1)
                    if pair >= 2:
                        act.wait_ge(values_ready, 2 * (pair - 1))
                    act.activation(v_hi[:, kv_slot(pair), :, :].rearrange("p a b -> p (a b)"), ps[:, PROJ + j % 2, :],
                                   ACT.Copy).then_inc(job_hi, 1)
                elif e[0] == "exp":
                    n = e[1]
                    pair, side, i, first, width = keys_of(n)
                    act.wait_ge(shift_ready, n + 1)
                    probs = s_buf[:, n % 3, 0:width]
                    act.activation(probs, probs, ACT.Exp, bias=shift[:, n:n + 1],
                                   accum_out=total[:, n:n + 1]).then_inc(exp_ready, 1)
                    if group_of(pair) == GROUP_C:
                        h = head_of(pair, side)
                        act.activation(sink_e[:, n:n + 1], sink[:, h:h + 1], ACT.Exp,
                                       bias=shift[:, n:n + 1]).then_inc(sink_ready, 1)
                elif e[0] == "keep":
                    n = e[1]
                    width = keys_of(n)[4]
                    act.wait_ge(turned, n + 1)
                    if n >= 8 and n % 4 == 0:
                        act.wait_ge(values_ready, n // 4 - 1)
                    act.activation(pt_blocks(pt_hi, n), ps[:, TURN + n % 2, 0:width].rearrange("p (j c) -> p j c", c=P),
                                   ACT.Copy).then_inc(kept_hi, 1)
                elif e[0] == "gather":
                    h = e[1]
                    pair, r = h // 2, HEAD_DIM * (h % 2)
                    act.wait_ge(values_ready, h + 1)
                    if pair >= MIX_SLOTS:
                        act.wait_ge(job_done, job_of["out", group_of(pair - MIX_SLOTS), 1, NT - 1] + 1)
                    head_out = ps[r:r + HEAD_DIM, VALUE + h % 2, :]
                    act.activation(mix_hi[r:r + HEAD_DIM, pair % MIX_SLOTS, :], head_out, ACT.Copy,
                                   scale=mix_g[r:r + HEAD_DIM, pair:pair + 1]).then_inc(gathered_hi, 1)
                    if h >= 4 and h % 4 == 0:
                        act.wait_ge(stats_done, h // 4)
                    act.activation(sq[r:r + HEAD_DIM, pair % 2, :], head_out, ACT.Square).then_inc(gathered_hi, 1)
            with act.Fori(0, FC // 2) as it:
                for b in range(2):
                    for part in range(2):
                        u = U_MLP + 2 * b + part + SPLIT - 1
                        act.wait_ge(raw_landed[u % RAW], it * 16 + 16 * (u // RAW + 1))
                        act.wait_ge(job_done, it * 4 + (JOBS + u - SPLIT - U_MLP + 1))
                        act.activation(w_hi[:, u % SPLIT, :], raw[:, u % RAW, :], ACT.Copy).then_inc(split_hi, 1)
                        if part == 0:
                            act.wait_ge(job_done, it * 4 + (JOBS + 2 * b + 1))
                            act.wait_ge(bank_drained, it * 2 + (JOBS + b - 1))
                            act.activation(act_g[:, b, :], ps[:, PROJ + b, :], ACT.Silu).then_inc(silu_ready, 1)
                    act.wait_ge(bank_drained, it * 2 + (JOBS + b + 1))
                    act.activation(gu_hi[:, it * 2 + b, :], gated[:, b, :], ACT.Copy).then_inc(gu_hi_ready, 1)
            for u in range(U_DOWN + SPLIT - 1, N_UNITS):
                landed(act, u)
                act.wait_ge(job_done, JOBS + u - SPLIT - U_MLP + 1)
                act.activation(w_hi[:, u % SPLIT, :], raw[:, u % RAW, :], ACT.Copy).then_inc(split_hi, 1)
            for m in range(2 * NT):
                t, half = m // 2, m % 2
                act.wait_ge(added, m + 1)
                act.activation(ps[:, m, :], xs[:, t, half * SEQ:(half + 1) * SEQ], ACT.Square,
                               accum_out=ssq_out[:, t, half:half + 1]).then_inc(squared, 1)

        @block.vector
        def _(dve):
            def split(u):
                dve.wait_ge(split_hi, u + 1)
                dve.tensor_tensor(w_lo[:, u % SPLIT, :], raw[:, u % RAW, :], as_f32(w_hi[:, u % SPLIT, :]),
                                  ALU.subtract).then_inc(split_lo, 1)

            z, soft, log_f, c = (s_buf[0:4, k, :] for k in (0, 1, 2, 0))
            decay_steps = [0]

            def step(ins):
                decay_steps[0] += 1
                ins.then_inc(decay_step, 1)
                dve.wait_ge(decay_step, decay_steps[0])

            for e in EVENTS:
                if e[0] == "split":
                    split(e[1])
                elif e[0] == "scale":
                    _, which, t = e
                    if t >= 2:
                        dve.wait_ge(rows_turned, 2 * (NT * which + t - 1))
                    dve.wait_ge(rstd_ready, NT * which + t + 1)
                    dve.wait_ge(gain_landed, 16 * (which + 1))
                    dve.scalar_tensor_tensor(tb[:, t % 2, :], xs[:, t, :], rstd[:, which, t:t + 1], gain[:], ALU.mult,
                                             ALU.mult).then_inc(scaled, 1)
                elif e[0] == "drain_h":
                    _, which, t = e
                    for half in range(2):
                        ks, ts = slice(4 * half, 4 * half + 4), slice(t * P, (t + 1) * P)
                        dve.wait_ge(rows_hi, 2 * (NT * which + t) + half + 1)
                        dve.tensor_tensor(h_lo[:, ks, ts], ps[:, TURN + half, :].rearrange("p (k c) -> p k c", k=4),
                                          as_f32(h_hi[:, ks, ts]), ALU.subtract).then_inc(rows_kept, 1)
                elif e[0] == "drain_table":
                    _, part, j = e
                    at, width = (0, SEQ) if part == 0 else (SEQ, ROW - SEQ)
                    dve.wait_ge(table_landed, 48)
                    dve.wait_ge(job_done, j + 1)
                    dve.tensor_tensor(rows[:, at:at + width], ps[0:BIAS_HEADS, PROJ + j % 2, 0:width],
                                      rows[:, at:at + width], ALU.add).then_inc(bank_drained, 1)
                elif e[0] == "drain" and e[1] in "qk":
                    _, kind, pair, j = e
                    hi, lo, slot = (q_hi, q_lo, pair % 2) if kind == "q" else (k_hi, k_lo, kv_slot(pair))
                    dve.wait_ge(job_hi, hi_upto[j])
                    dve.scalar_tensor_tensor(by_tiles(lo[:, slot, :]), projected(kind, j), SCALE if kind == "q" else 1.0,
                                             by_tiles(as_f32(hi[:, slot, :])), ALU.mult, ALU.subtract).then_inc(bank_drained, 1)
                elif e[0] == "drain" and e[1] == "v":
                    _, _, pair, j = e
                    if pair == 0:
                        dve.wait_ge(rows_stored, 16)
                    dve.wait_ge(job_done, j + 1)
                    dve.tensor_copy(vt[:, pair % 2, :], ps[:, PROJ + j % 2, :]).then_inc(bank_drained, 1)
                elif e[0] == "drain" and e[1] == "f":
                    j = e[3]
                    dve.wait_ge(job_done, j + 1)
                    dve.wait_ge(const_landed, 64)
                    dve.tensor_scalar(z, ps[0:4, PROJ + j % 2, :], fb[:, 0:1], None, ALU.add).then_inc(bank_drained, 1)
                    dve.wait_ge(bank_drained, j + 1)
                    step(dve.scalar_tensor_tensor(soft, z, -1.0, z, ALU.mult, ALU.max))
                elif e[0] == "decays" and e[1] == 1:
                    dve.wait_ge(softplus_ready, 2)
                    step(dve.scalar_tensor_tensor(log_f, z, 0.0, soft, ALU.min, ALU.subtract))
                    dve.wait_ge(consts_ready, 10)
                    step(dve.tensor_tensor_scan(c, log_f, zero_row[:], 0.0, ALU.add, ALU.add))
                elif e[0] == "decays" and e[1] == 2:
                    step(dve.tensor_scalar(decay[0:4, :], c, -1.0, None, ALU.mult))
                    step(dve.tensor_scalar(decay[64:68, :], c, -1.0, None, ALU.mult))
                elif e[0] == "decays" and e[1] == 3:
                    for r in (32, 96):
                        step(dve.scalar_tensor_tensor(decay[r:r + 4, :], c, -1.0, as_f32(decay[0:4, :]), ALU.mult,
                                                      ALU.subtract))
                    step(dve.tensor_copy(pick_r[:], pick_f[:]))
                elif e[0] == "drain_v":
                    _, pair, j = e
                    slot = kv_slot(pair)
                    dve.wait_ge(job_hi, hi_upto[j])
                    dve.tensor_tensor(v_lo[:, slot, :, :].rearrange("p a b -> p (a b)"), ps[:, PROJ + j % 2, :],
                                      as_f32(v_hi[:, slot, :, :]).rearrange("p a b -> p (a b)"),
                                      ALU.subtract).then_inc(bank_drained, 1)
                elif e[0] == "max":
                    n = e[1]
                    pair, side, i, first, width = keys_of(n)
                    dve.wait_ge(scores_ready, n + 1)
                    if n % 8 == 0:
                        dve.wait_ge(bias_landed[pair % 2], 16 * (pair // 2 + 1))
                    if n >= 3:
                        dve.wait_ge(turned, n - 2)
                    least = sink[:, head_of(pair, side):head_of(pair, side) + 1] if group_of(pair) == GROUP_C else LOWEST
                    end = SEQ * (side + 1)
                    dve.tensor_tensor_reduce(s_buf[:, n % 3, 0:width], ps[:, SCORE + n % 2, 0:width],
                                             tb[:, pair % 2, end - width:end], 1.0, least, ALU.add, ALU.max,
                                             top[:, n:n + 1]).then_inc(top_ready, 1)
                    dve.wait_ge(top_ready, n + 1)
                    dve.tensor_scalar(shift[:, n:n + 1], top[:, n:n + 1], -1.0, None, ALU.mult).then_inc(shift_ready, 1)
                elif e[0] == "norm":
                    n = e[1]
                    dve.wait_ge(exp_ready, n + 1)
                    sums = total
                    if group_of(n // 8) == GROUP_C:
                        dve.wait_ge(sink_ready, n - 8 * 6 + 1)
                        dve.tensor_tensor(total2[:, n:n + 1], total[:, n:n + 1], sink_e[:, n:n + 1],
                                          ALU.add).then_inc(total_ready, 1)
                        dve.wait_ge(total_ready, n - 8 * 6 + 1)
                        sums = total2
                    dve.reciprocal(inv[:, n:n + 1], sums[:, n:n + 1]).then_inc(inv_ready, 1)
                elif e[0] == "keep":
                    n = e[1]
                    width = keys_of(n)[4]
                    dve.wait_ge(kept_hi, n + 1)
                    dve.tensor_tensor(pt_blocks(pt_lo, n), ps[:, TURN + n % 2, 0:width].rearrange("p (j c) -> p j c", c=P),
                                      as_f32(pt_blocks(pt_hi, n)), ALU.subtract).then_inc(kept_lo, 1)
                elif e[0] == "gather":
                    h = e[1]
                    pair, r = h // 2, HEAD_DIM * (h % 2)
                    dve.wait_ge(gathered_hi, 2 * (h + 1))
                    dve.scalar_tensor_tensor(mix_lo[r:r + HEAD_DIM, pair % MIX_SLOTS, :],
                                             ps[r:r + HEAD_DIM, VALUE + h % 2, :], mix_g[r:r + HEAD_DIM, pair:pair + 1],
                                             as_f32(mix_hi[r:r + HEAD_DIM, pair % MIX_SLOTS, :]), ALU.mult,
                                             ALU.subtract).then_inc(gathered_lo, 1)
                elif e[0] == "stats":
                    g = e[1]
                    dve.wait_ge(stats_done, g + 1)
                    dve.tensor_scalar(g_mean[:, g, :], by_tiles(ps[:, VALUE + 1, :])[:, :, 0],
                                      1.0 / (4 * HEAD_DIM), EPS, ALU.mult, ALU.add).then_inc(g_mean_ready, 1)
                elif e[0] == "drain_out":
                    _, g, half, t, j = e
                    cols = slice(half * SEQ, (half + 1) * SEQ)
                    dve.wait_ge(job_done, j + 1)
                    dve.wait_ge(g_rstd_ready, g + 1)
                    dve.wait_ge(bank_drained, j)
                    dve.scalar_tensor_tensor(xs[:, t, cols], ps[:, PROJ + j % 2, :], g_rstd[:, g, t:t + 1],
                                             xs[:, t, cols], ALU.mult, ALU.add).then_inc(bank_drained, 1)
            with dve.Fori(0, FC // 2) as it:
                for b in range(2):
                    for part in range(2):
                        u = U_MLP + 2 * b + part + SPLIT - 1
                        dve.wait_ge(split_hi, it * 4 + (u + 1))
                        dve.tensor_tensor(w_lo[:, u % SPLIT, :], raw[:, u % RAW, :], as_f32(w_hi[:, u % SPLIT, :]),
                                          ALU.subtract).then_inc(split_lo, 1)
                    dve.wait_ge(silu_ready, it * 2 + (b + 1))
                    dve.wait_ge(job_done, it * 4 + (JOBS + 2 * b + 2))
                    dve.tensor_tensor(gated[:, b, :], ps[:, SCORE + b, :], act_g[:, b, :],
                                      ALU.mult).then_inc(bank_drained, 1)
                    dve.wait_ge(gu_hi_ready, it * 2 + (b + 1))
                    dve.tensor_tensor(gu_lo[:, it * 2 + b, :], gated[:, b, :], as_f32(gu_hi[:, it * 2 + b, :]),
                                      ALU.subtract).then_inc(gu_lo_ready, 1)
            for u in range(U_DOWN + SPLIT - 1, N_UNITS):
                split(u)

            def add_down(m):
                at = (slice(None), m // 2, slice(m % 2 * SEQ, (m % 2 + 1) * SEQ))
                dve.wait_ge(down_done, m + 1)
                dve.tensor_tensor(xs[at], ps[:, m, :], xs[at], ALU.add).then_inc(added, 1)

            dve.wait_ge(gain_landed, 16 * 3)
            for t in range(NT + 1):
                if t < NT:
                    add_down(2 * t)
                for half in range(2):
                    if t >= 1:
                        at = (slice(None), t - 1, slice(half * SEQ, (half + 1) * SEQ))
                        dve.wait_ge(rstd_ready, 2 * NT + t)
                        dve.scalar_tensor_tensor(xs[at], xs[at], rstd[:, 2, t - 1:t], gain[:, at[2]], ALU.mult,
                                                 ALU.mult).then_inc(scaled, 1)
                if t < NT:
                    add_down(2 * t + 1)

        @block.tensor
        def _(pe):
            def thrice(bank, a, b, first, last):
                pe.matmul(bank, a[0], b[0], start=first, stop=False)
                pe.matmul(bank, a[0], b[1], start=False, stop=False)
                return pe.matmul(bank, a[1], b[0], start=False, stop=last)

            def gate_or_up(part, b, u, tokens):
                for k in range(NK):
                    cols = slice(k * P, (k + 1) * P)
                    mm = thrice(ps[:, 2 * part + b, tokens], (w_hi[:, u % SPLIT, cols], w_lo[:, u % SPLIT, cols]),
                                (h_hi[:, k, tokens], h_lo[:, k, tokens]), k == 0, k == NK - 1)
                return mm

            def bank_free(j):
                if j >= 2:
                    pe.wait_ge(bank_drained, j - 1)

            pe.wait_ge(consts_ready, 1)
            for _ in range(WARM_UP):
                pe.matmul(ps[:, SCORE, 0:P], ones[:], ones[:], start=True, stop=True)
            for e in EVENTS:
                if e[0] == "table":
                    _, part, j = e
                    at, width = (0, SEQ) if part == 0 else (SEQ, ROW - SEQ)
                    pe.wait_ge(table_landed, 48)
                    pe.matmul(ps[0:BIAS_HEADS, PROJ + j % 2, 0:width], table[:], hot[:, at:at + width], start=True,
                              stop=True).then_inc(job_done, 1)
                elif e[0] == "turn_h":
                    _, which, t = e
                    if which == 0:
                        pe.wait_ge(consts_ready, 3)
                    pe.wait_ge(scaled, NT * which + t + 1)
                    for half in range(2):
                        if NT * which + t >= 1:
                            pe.wait_ge(rows_kept, 2 * (NT * which + t) + half - 1)
                        for k in range(4):
                            at = (4 * half + k) * P
                            mm = pe.transpose(ps[:, TURN + half, k * P:(k + 1) * P], tb[:, t % 2, at:at + P], ident[:])
                        mm.then_inc(rows_turned, 1)
                elif e[0] == "piece":
                    _, kind, u, j, ks, tokens = e
                    if ks[0] == 0:
                        bank_free(j)
                        pe.wait_ge(split_lo, u + 1)
                        pe.wait_ge(rows_kept, 2 * tokens.stop // P)
                    for k in ks:
                        cols = slice(k * P, (k + 1) * P)
                        mm = thrice(ps[:, PROJ + j % 2, tokens], (w_hi[:, u % SPLIT, cols], w_lo[:, u % SPLIT, cols]),
                                    (h_hi[:, k, tokens], h_lo[:, k, tokens]), k == 0, k == NK - 1)
                    if ks[-1] == NK - 1 and tokens.stop == SEQ:
                        mm.then_inc(job_done, 1)
                elif e[0] == "turn_v":
                    _, pair, j = e
                    bank_free(j)
                    pe.wait_ge(bank_drained, job_of["v", pair] + 1)
                    for t in range(NT):
                        ts = slice(t * P, (t + 1) * P)
                        mm = pe.transpose(ps[:, PROJ + j % 2, ts], vt[:, pair % 2, ts], ident[:])
                    mm.then_inc(job_done, 1)
                elif e[0] == "scores":
                    n = e[1]
                    pair, side, i, first, width = keys_of(n)
                    r, qs = slice(HEAD_DIM * side, HEAD_DIM * side + HEAD_DIM), slice(i * P, (i + 1) * P)
                    ks = slice(first, first + max(width, 2 * P))
                    if n % 8 == 0:
                        pe.wait_ge(bank_drained, max(job_of["q", pair], job_of["k", pair]) + 1)
                    if n == 0:
                        pe.wait_ge(decay_step, 8)
                    if n >= 2:
                        pe.wait_ge(top_ready, n - 1)
                    bank, a, kv = ps[:, SCORE + n % 2, 0:ks.stop - ks.start], pair % 2, kv_slot(pair)
                    of_d = group_of(pair) == GROUP_D
                    mm = thrice(bank, (q_hi[r, a, qs], q_lo[r, a, qs]), (k_hi[r, kv, ks], k_lo[r, kv, ks]), True, not of_d)
                    if of_d:
                        mm = pe.matmul(bank, pick_r[r, head_of(pair, side), :], decay[r, ks], start=False, stop=True)
                    mm.then_inc(scores_ready, 1)
                elif e[0] == "turn":
                    n = e[1]
                    pe.wait_ge(probs_ready, n + 1)
                    if n >= 2:
                        pe.wait_ge(kept_lo, n - 1)
                    for k in range(keys_of(n)[4] // P):
                        ks = slice(k * P, (k + 1) * P)
                        mm = pe.transpose(ps[:, TURN + n % 2, ks], s_buf[:, n % 3, ks], mirror[:])
                    mm.then_inc(turned, 1)
                elif e[0] == "values":
                    h = e[1]
                    pair, slot = h // 2, kv_slot(h // 2)
                    banded = group_of(pair) == GROUP_C
                    pe.wait_ge(kept_lo, 4 * (h + 1))
                    if h % 2 == 0:
                        pe.wait_ge(bank_drained, job_of["v_turned", pair] + 1)
                    if h >= 2:
                        pe.wait_ge(gathered_lo, h - 1)
                    if h % 4 == 1 and h > 4:
                        pe.wait_ge(g_mean_ready, h // 4)
                    if banded and h < 14:
                        pe.wait_ge(zeros_ready, 2 * (h - 11))
                    for k in range(NT):
                        q0, q1 = (min(k, 2), NT if k == 0 or not banded else min(k + 2, NT))
                        moving = slice(PT_STRIDE * k + P * q0, PT_STRIDE * k + P * q1)
                        mm = thrice(ps[:, VALUE + h % 2, P * q0:P * q1], (v_hi[:, slot, k, :], v_lo[:, slot, k, :]),
                                    (pt_hi[:, h % 2, moving], pt_lo[:, h % 2, moving]), k == 0, k == NT - 1)
                    mm.then_inc(values_ready, 1)
                elif e[0] == "stats":
                    g = e[1]
                    pe.wait_ge(gathered_lo, 4 * (g + 1))
                    pe.wait_ge(squares_added, g + 1)
                    for t in range(NT):
                        ts = slice(t * P, (t + 1) * P)
                        mm = pe.matmul(ps[:, VALUE + 1, ts], sq[:, 0, ts], ones[:], start=True, stop=True)
                    mm.then_inc(stats_done, 1)
                elif e[0] == "out":
                    _, g, half, t, u, j = e
                    bank_free(j)
                    if t == 0:
                        pe.wait_ge(split_lo, u + 1)
                        pe.wait_ge(gathered_lo, 4 * (g + 1))
                    ts = slice(t * P, (t + 1) * P)
                    for c in range(2):
                        slot, cols = (2 * g + c) % MIX_SLOTS, slice(c * SEQ, (c + 1) * SEQ)
                        mm = thrice(ps[:, PROJ + j % 2, :], (mix_hi[:, slot, ts], mix_lo[:, slot, ts]),
                                    (w_hi[:, u % SPLIT, cols], w_lo[:, u % SPLIT, cols]), c == 0, c == 1)
                    mm.then_inc(job_done, 1)
                elif e[0] == "mlp":
                    _, part, half = e
                    u, tokens = U_MLP + part, slice(half * SEQ // 2, (half + 1) * SEQ // 2)
                    pe.wait_ge(split_lo, u + 1)
                    pe.wait_ge(bank_drained, JOBS)
                    pe.wait_ge(top_ready, STEPS)
                    pe.wait_ge(rows_kept, 2 * (NT + tokens.stop // P))
                    mm = gate_or_up(part, 0, u, tokens)
                    if half == 1:
                        mm.then_inc(job_done, 1)

            def features(it, tiles):
                for b in tiles:
                    for part in range(2):
                        u = U_MLP + 2 * b + part
                        pe.wait_ge(split_lo, it * 4 + (u + 1))
                        if part == 0:
                            pe.wait_ge(bank_drained, it * 2 + (JOBS + b - 1))
                        gate_or_up(part, b, u, slice(0, SEQ)).then_inc(job_done, 1)

            features(0, [1])
            with pe.Fori(1, FC // 2) as it:
                features(it, range(2))
            pe.wait_ge(bank_drained, JOBS + FC)
            def down(f, t, half):
                ts, cols, u = slice(t * P, (t + 1) * P), slice(half * SEQ, (half + 1) * SEQ), U_DOWN + f
                return thrice(ps[:, 2 * t + half, :], (gu_hi[:, f, ts], gu_lo[:, f, ts]),
                              (w_hi[:, u % SPLIT, cols], w_lo[:, u % SPLIT, cols]), f == 0, f == FC - 1)

            def down_ready(f):
                pe.wait_ge(split_lo, U_DOWN + f + 1)
                pe.wait_ge(gu_lo_ready, f + 1)

            for f in range(FC - 2):
                down_ready(f)
                for t in range(NT):
                    down(f, t, 0)
                    mm = down(f, t, 1)
                mm.then_inc(job_done, 1)
            down_ready(FC - 2)
            down_ready(FC - 1)
            for m in range(2 * NT):
                down(FC - 2, m // 2, m % 2)
                down(FC - 1, m // 2, m % 2).then_inc(down_done, 1)



def weight_units(w_in, w_out, w_gate, w_up, w_down):
    def tiles(w):
        w = np.pad(w, ((0, 0), (0, P - w.shape[1])))
        return w.reshape(NK, P, P).transpose(1, 0, 2).reshape(P, UNIT)

    def heads(pair):
        return [head_of(pair, side) for side in range(2)]

    def columns(start, picked):
        return np.concatenate([w_in[:, start + h * HEAD_DIM:start + (h + 1) * HEAD_DIM] for h in picked], axis=1)

    units = {}
    for e in plan()[0]:
        if e[0] == "piece":
            units[e[2]] = (e[1],)
        if e[0] == "out" and e[3] == 0:
            _, g, half, _, u, _ = e
            rows = []
            for pair in (2 * g, 2 * g + 1):
                at = [MIX_AT[g] + h * HEAD_DIM for h in heads(pair)]
                rows.append(np.concatenate([w_out[a:a + HEAD_DIM, half * SEQ:(half + 1) * SEQ] for a in at]))
            units[u] = np.concatenate(rows, axis=1)
    pending = [u for u in sorted(units) if isinstance(units[u], tuple)]
    seen = {"q": 0, "k": 0, "v": 0}
    for u in pending:
        kind = units[u][0]
        if kind == "f":
            units[u] = tiles(w_in[:, F_AT:F_AT + 4])
            continue
        pair = seen[kind]
        seen[kind] += 1
        g = group_of(pair)
        if kind == "q":
            units[u] = tiles(columns(Q_AT[g], heads(pair)))
        else:
            picked = [0, 1] if g == GROUP_C else heads(pair)
            units[u] = tiles(columns((K_AT if kind == "k" else V_AT)[g], picked))
    out = [units[u] for u in range(len(units))]
    for f in range(FC):
        out += [tiles(w_gate[:, f * P:(f + 1) * P]), tiles(w_up[:, f * P:(f + 1) * P])]
    out += [w_down[f * P:(f + 1) * P, :] for f in range(FC)]
    return np.stack(out)


def kernel(x, norm1_g, w_in, f_bias, sinks, mix_norm_g, w_out, norm2_g, w_gate, w_up, w_down, rel_bias, final_g):
    import concourse.bacc as bacc
    from concourse.bass_utils import run_bass_kernel_spmd

    arrays = [np.asarray(a) for a in (x, norm1_g, w_in, f_bias, sinks, mix_norm_g, w_out, norm2_g, w_gate, w_up,
                                      w_down, rel_bias, final_g)]
    x, norm1_g, w_in, f_bias, sinks, mix_norm_g, w_out, norm2_g, w_gate, w_up, w_down, rel_bias, final_g = arrays
    onehot, band_add, pick = band_constants()
    mix_gain = np.stack([np.concatenate([mix_norm_g[0, MIX_AT[group_of(p)] + h * HEAD_DIM:][:HEAD_DIM]
                                         for h in (head_of(p, 0), head_of(p, 1))]) for p in range(PAIRS)], axis=1)
    ins = {
        "x": x[0],
        "units": weight_units(w_in[0], w_out[0], w_gate[0], w_up[0], w_down[0]),
        "gains": np.stack([norm1_g[0], norm2_g[0], final_g]),
        "mix_gain": mix_gain,
        "f_bias": f_bias.reshape(4, 1),
        "sinks": np.broadcast_to(sinks, (P, 4)),
        "rel_bias": rel_bias,
        "onehot": onehot,
        "band_add": band_add,
        "pick": pick,
    }
    ins = {f"in_{name}": np.ascontiguousarray(a) for name, a in ins.items()}
    nc = bacc.Bacc("TRN2", target_bir_lowering=False, num_devices=1)
    args = [nc.dram_tensor(name, a.shape, mybir.dt.from_np(a.dtype), kind="ExternalInput").ap() for name, a in ins.items()]
    out = nc.dram_tensor("out", (SEQ, D_MODEL), F32, kind="ExternalOutput").ap()
    hybrid_layer(nc, *args, out)
    r = run_bass_kernel_spmd(nc, [ins], core_ids=[0])
    return np.asarray(r.results[0]["out"]).reshape(1, SEQ, D_MODEL)
```

```python
from contextlib import ExitStack

import numpy as np
import concourse.bass as bass
from concourse import mybir

F32 = mybir.dt.float32
F32R = mybir.dt.float32r
ALU = mybir.AluOpType
ACT = mybir.ActivationFunctionType

P = 128
SEQ = 512
D_MODEL = 1024
HEAD_DIM = 64
N_BUCKETS = 32
T5_MAX_DISTANCE = 2048
D_FF = 2816
EPS = 1e-6
NEG = -1e30
SCALE = HEAD_DIM ** -0.5
LOWEST = -3.0e38

NT = SEQ // P
NK = D_MODEL // P
FC = D_FF // P
PAIRS = 8
STEPS = 8 * PAIRS
GROUP_D, GROUP_A, GROUP_B, GROUP_C = range(4)
RAW = 4
SPLIT = 4
UNIT = NK * P
MIX_SLOTS = 6
MIX_AT = [768, 0, 256, 512]
Q_AT = [2048, 0, 768, 1536]
K_AT = [2304, 256, 1024, 1792]
V_AT = [2560, 512, 1280, 1920]
F_AT = 2816
F_COLS = 36
ROW = 640
BIAS_HEADS = 12
MASK_ROW = BIAS_HEADS
WARM_UP = 20
TOGETHER = 3
PIECE = 2
SPLIT_AT = 1
ORDER = [
    ("scores", 0), ("norm", 1), ("max", 0), ("turn", 2), ("gather_lo", 5), ("values", 3), ("gather_hi", 5),
    ("fill", 0), ("keep_hi", 2), ("stats", 7), ("keep_lo", 2), ("stats_mean", 8), ("sum", 3), ("fill", 0),
    ("exp", 0)
]
OUT_PAIRS = [4, 5, 6, 6, 7, 7]
PIECES = [14, 14, 12, 14, 14, 18, 14, 6]
LEAD = 3
C_AT = 3
PT_STRIDE = 384
PT_WIDTH = 3 * PT_STRIDE + SEQ


def group_of(pair):
    return pair // 2


def head_of(pair, side):
    c = pair % 2
    return c + 2 * side if group_of(pair) == GROUP_C else 2 * c + side


def keys_of(n):
    pair, side, i = n // 8, n // 4 % 2, n % 4
    first = P * (i - 1) if group_of(pair) == GROUP_C and i else 0
    return pair, side, i, first, P * (i + 1) - first


def kv_slot(pair):
    return pair % 2 if pair < 7 else 0


def plan():
    events, unit_job, count = [], {}, {"job": 0, "unit": 0}
    emitted = {"scores": 0, "values": 0}

    def job():
        count["job"] += 1
        return count["job"] - 1

    def next_unit():
        u = count["unit"]
        count["unit"] += 1
        return u

    def ahead(u):
        events.append(("split", u + SPLIT - 1))
        events.append(("load", u + SPLIT - 1 + RAW))

    def projection(kind, pair):
        u, j = next_unit(), job()
        unit_job[u] = j
        for r in range(NK // PIECE):
            events.append(("piece", kind, u, j, range(PIECE * r, PIECE * (r + 1)), slice(0, SEQ)))
            if r == SPLIT_AT:
                ahead(u)
            yield
        while kind in "qk" and emitted["scores"] < 8 * (pair - 1):
            yield
        events.append(("drain", kind, pair, j))
        if kind == "k":
            events.append(("repeat_keys", pair, j))

    def turn_values(pair):
        while emitted["values"] < 2 * (pair - 1):
            yield
        h = emitted["values"]
        events.append(("turn_v", pair, h))
        events.append(("drain_v", pair, h))
        yield

    def projections(pair):
        if pair == 7:
            return projection("q", pair)
        return chain(projection("v", pair), projection("k", pair), turn_values(pair), projection("q", pair))

    def output(group, half):
        u = next_unit()
        for t in range(NT):
            j = job()
            unit_job[u] = j
            events.append(("out", group, half, t, u, j))
            if t == 1:
                ahead(u)
            yield
            events.append(("drain_out", group, half, t, j))

    def chain(*parts):
        for part in parts:
            yield from part

    def run(filler):
        for _ in filler:
            pass

    def normed(which, *stages):
        for stage, t in stages:
            events.append((stage, which, t))

    for u in range(RAW):
        events.append(("load", u))
    f_u, f_j, v_u, v_j = next_unit(), job(), next_unit(), job()
    unit_job[f_u], unit_job[v_u] = f_j, v_j

    def half_product(kind, u, j, half):
        events.append(("piece", kind, u, j, range(NK), slice(half * SEQ // 2, (half + 1) * SEQ // 2)))

    def split_and_load(u):
        events.append(("split", u))
        events.append(("load", u + RAW))

    normed(0, ("square", 0), ("root", 0), ("square", 1), ("root", 1), ("scale", 0), ("turn_h", 0), ("scale", 1),
           ("square", 2), ("root", 2), ("drain_h", 0), ("turn_h", 1), ("scale", 2), ("square", 3), ("root", 3),
           ("drain_h", 1))
    split_and_load(0)
    events.append(("table",))
    normed(0, ("turn_h", 2), ("scale", 3), ("drain_h", 2))
    half_product("f", f_u, f_j, 0)
    split_and_load(1)
    normed(0, ("turn_h", 3), ("drain_h", 3))
    half_product("v", v_u, v_j, 0)
    split_and_load(2)
    events.append(("drain_table",))
    events.append(("store_rows",))
    half_product("f", f_u, f_j, 1)
    half_product("v", v_u, v_j, 1)
    events.append(("drain", "f", 0, f_j))
    ahead(f_u)
    ahead(v_u)
    events.append(("drain", "v", 0, v_j))
    events.append(("bias", 0))
    events.append(("bias", 1))
    decays = iter(range(4))
    for _ in chain(projection("k", 0), turn_values(0), projection("q", 0)):
        events.extend(("decays", stage) for stage in [next(decays, None)] if stage is not None)

    fillers = [projections(pair + 1) for pair in range(PAIRS - 1)] + [chain()]
    for n, pair in enumerate(OUT_PAIRS):
        fillers[pair] = chain(fillers[pair], output(n // 2, n % 2))

    def fill(slot):
        pair, at = slot // 16, slot % 16
        if pair >= PAIRS:
            next(fillers[-1], None)
            return
        share = PIECES[pair] / 16
        for _ in range(int(share * (at + 1) + 1e-6) - int(share * at + 1e-6)):
            next(fillers[pair], None)
        if at == 15 and pair < PAIRS - 1:
            run(fillers[pair])

    c_units = []
    for slot in range(LEAD):
        fill(slot)
    for s in range(STEPS + 6):
        fills = 0
        for stage, lag in ORDER:
            n = s - lag
            if stage == "fill":
                fill(2 * s + LEAD + fills)
                fills += 1
            elif not 0 <= n < STEPS:
                continue
            elif stage in ("values", "sum", "gather_hi", "gather_lo"):
                if n % 4 == 3:
                    events.append((stage, n // 4))
            elif stage in ("stats", "stats_mean"):
                if n % 16 == 15 and n // 16 < GROUP_C:
                    events.append((stage, n // 16))
            else:
                events.append((stage, n))
            if stage in ("scores", "values") and events[-1][0] == stage:
                emitted[stage] = events[-1][1] + 1
        if s % 8 == 2 and 2 <= s // 8 + 1 < PAIRS:
            events.append(("bias", s // 8 + 1))
        if s == STEPS // 2:
            events.append(("gain", 1))
        if s == STEPS + C_AT:
            run(fillers[-1])
            for part in range(2):
                c_units.append(next_unit())
            events.append(("out_begin", c_units))

    def out_tile(t):
        for half in range(2):
            events.append(("out_c", half, t, c_units[half]))

    def add_tile(t):
        for half in range(2):
            events.append(("add_c", half, t))

    ahead(c_units[0])
    events.append(("stats_end",))
    events.append(("stats_mean", GROUP_C))
    out_tile(0)
    out_tile(1)
    add_tile(0)
    add_tile(1)
    normed(1, ("square", 0), ("root", 0), ("square", 1), ("root", 1))
    out_tile(2)
    add_tile(2)
    normed(1, ("scale", 0), ("scale", 1), ("square", 2), ("root", 2))
    out_tile(3)
    add_tile(3)
    normed(1, ("turn_h", 0), ("drain_h", 0), ("square", 3), ("root", 3), ("turn_h", 1), ("scale", 2), ("drain_h", 1),
           ("turn_h", 2), ("scale", 3), ("drain_h", 2))
    events.append(("mlp", 0, 0))
    normed(1, ("turn_h", 3), ("drain_h", 3))
    ahead(c_units[1])
    events.append(("mlp", 1, 0))
    events.append(("mlp", 0, 1))
    events.append(("mlp", 1, 1))
    return events, unit_job, count["job"], count["unit"]


def band_constants():
    dist = SEQ - 1 - np.arange(ROW)
    n = np.maximum(dist, 0)
    exact = N_BUCKETS // 2
    large = exact + (np.log(np.maximum(n, 1) / exact) / np.log(T5_MAX_DISTANCE / exact)
                     * (N_BUCKETS - exact)).astype(np.int64)
    bucket = np.where(n < exact, n, np.minimum(large, N_BUCKETS - 1))
    onehot = (np.arange(N_BUCKETS)[:, None] == bucket).astype(np.float32)
    causal = dist >= 0
    bands = (dist <= 128).astype(int) + (dist % 4 == 0) + (dist % 16 == 0)
    add = np.zeros((BIAS_HEADS + 1, ROW), np.float32)
    add[0:4] = np.where(causal & (bands > 0), np.log(np.maximum(bands, 1)), NEG)
    add[4:8] = np.where(causal, 0.0, NEG)
    add[8:12] = np.where(causal & (dist < 128), 0.0, NEG)
    add[MASK_ROW] = np.where(causal, 0.0, NEG)
    pick = np.zeros((P, 4, P), np.float32)
    for h in range(4):
        pick[h::32, h] = 1.0
    return onehot, add, pick


def hybrid_layer(nc, x, units, gains, mix_gain, f_bias, sinks, rel_bias, onehot, band_add, pick, out):
    EVENTS, UNIT_JOB, JOBS, U_MLP = plan()
    U_DOWN = U_MLP + 2 * FC
    N_UNITS = U_DOWN + FC
    hi_upto, job_of, hi_count = {}, {}, 0
    for e in EVENTS:
        if e[0] == "drain" and e[1] in "qk":
            hi_count += 1
            hi_upto[e[-1]] = hi_count
        if e[0] == "drain":
            job_of[e[1], e[2]] = e[3]
        if e[0] == "out":
            job_of["out", e[1], e[2], e[3]] = e[5]
    for what in "kv":
        job_of[what, 7] = job_of[what, 6]

    bias_rows = nc.dram_tensor("bias_rows", (BIAS_HEADS, ROW), F32, kind="Internal")

    def skewed(rows, row, step):
        return bass.AP(tensor=rows, offset=row * ROW, ap=[[1, P], [step * ROW, 2], [1, SEQ]])

    with ExitStack() as ctx:
        def sb(name, shape, dt=F32, stack=ctx):
            return stack.enter_context(nc.sbuf_tensor(name, shape, dt))

        def sem(name):
            return ctx.enter_context(nc.semaphore(name))

        xs = sb("xs", [P, NT, D_MODEL])
        h_hi = sb("h_hi", [P, NK, SEQ], F32R)
        h_lo = sb("h_lo", [P, NK, SEQ], F32R)
        raw = sb("raw", [P, RAW, UNIT])
        w_hi = sb("w_hi", [P, SPLIT, UNIT], F32R)
        w_lo = sb("w_lo", [P, SPLIT, UNIT], F32R)
        gain = sb("gain", [P, D_MODEL])
        ident = sb("ident", [P, P])
        mirror = sb("mirror", [P, P])
        ones = sb("ones", [P, P])
        table = sb("table", [N_BUCKETS, BIAS_HEADS])
        mix_g = sb("mix_g", [P, PAIRS])
        fb = sb("fb", [4, 1])
        sink = sb("sink", [P, 4])
        minus_half = sb("minus_half", [P, NT])
        ssq = sb("ssq", [P, 2, NT])
        mean = sb("mean", [P, 3, NT])
        rstd = sb("rstd", [P, 3, NT])
        ssq_out = sb("ssq_out", [P, NT, 2])
        part_mean = sb("part_mean", [P, NT])
        g_mean = sb("g_mean", [P, 4, NT])
        g_rstd = sb("g_rstd", [P, 4, NT])
        top = sb("top", [P, STEPS])
        shift = sb("shift", [P, STEPS])
        total = sb("total", [P, STEPS])
        sink_e = sb("sink_e", [P, STEPS])
        total2 = sb("total2", [P, STEPS])
        inv = sb("inv", [P, STEPS])
        tb = sb("tb", [P, 2, 1024])
        attn = ctx.enter_context(ExitStack())
        q_both = sb("q_both", [P, 2, 2, SEQ], F32R, attn)
        k_twice = sb("k_twice", [P, 2, 2, SEQ], F32R, attn)
        k_lo = sb("k_lo", [P, 2, SEQ], F32R, attn)
        v_both = sb("v_both", [P, 2, NT, 2 * P], F32R, attn)
        pt_hi = sb("pt_hi", [P, 2, PT_WIDTH], F32R, attn)
        pt_lo = sb("pt_lo", [P, 2, PT_WIDTH], F32R, attn)
        mix_hi = sb("mix_hi", [P, MIX_SLOTS, SEQ], F32R, attn)
        mix_lo = sb("mix_lo", [P, MIX_SLOTS, SEQ], F32R, attn)
        decay = sb("decay", [P, SEQ], F32R, attn)
        pick_r = sb("pick_r", [P, 4, P], F32R, attn)
        head_sum = sb("head_sum", [P, SEQ], F32, attn)
        s_buf = sb("s_buf", [P, 3, SEQ], F32, attn)
        sq = sb("sq", [P, 2, SEQ], F32, attn)
        vt = sb("vt", [P, SEQ], F32, attn)
        attn.close()
        mlp = ctx.enter_context(ExitStack())
        gu_hi = sb("gu_hi", [P, FC, SEQ], F32R, mlp)
        gu_lo = sb("gu_lo", [P, FC, SEQ], F32R, mlp)
        act_g, gated = tb[:, :, 0:SEQ], tb[:, :, SEQ:2 * SEQ]
        hot = sq[0:N_BUCKETS, :, :].rearrange("p a b -> p (a b)")[:, 0:ROW]
        rows = s_buf[0:BIAS_HEADS, :, :].rearrange("p a b -> p (a b)")[:, 0:ROW]
        pick_f = head_sum[:].rearrange("p (h c) -> p h c", c=P)

        ps = ctx.enter_context(nc.psum_tensor("ps", [P, 8, SEQ], F32))
        PROJ, SCORE, TURN, VALUE = 0, 2, 4, 6

        x_landed = [sem(f"x_landed{t}") for t in range(NT)]
        gain_landed = sem("gain_landed")
        const_landed = sem("const_landed")
        table_landed = sem("table_landed")
        table_done = sem("table_done")
        rows_ready = sem("rows_ready")
        rows_stored = sem("rows_stored")
        values_turned = sem("values_turned")
        values_hi_ready = sem("values_hi_ready")
        values_kept = sem("values_kept")
        bias_landed = [sem(f"bias_landed{i}") for i in range(2)]
        raw_landed = [sem(f"raw_landed{i}") for i in range(RAW)]
        out_stored = sem("out_stored")
        consts_ready = sem("consts_ready")
        squared = sem("squared")
        mean_ready = sem("mean_ready")
        rstd_ready = sem("rstd_ready")
        scaled = sem("scaled")
        out_done = sem("out_done")
        out_added = sem("out_added")
        rows_turned = sem("rows_turned")
        rows_hi = sem("rows_hi")
        rows_kept = sem("rows_kept")
        job_done = sem("job_done")
        job_hi = sem("job_hi")
        bank_drained = sem("bank_drained")
        split_hi = sem("split_hi")
        split_lo = sem("split_lo")
        decay_step = sem("decay_step")
        softplus_ready = sem("softplus_ready")
        scores_ready = sem("scores_ready")
        top_ready = sem("top_ready")
        shift_ready = sem("shift_ready")
        exp_ready = sem("exp_ready")
        sink_ready = sem("sink_ready")
        total_ready = sem("total_ready")
        inv_ready = sem("inv_ready")
        probs_ready = sem("probs_ready")
        turned = sem("turned")
        kept_hi = sem("kept_hi")
        kept_lo = sem("kept_lo")
        values_ready = sem("values_ready")
        keys_repeated = sem("keys_repeated")
        low_copied = sem("low_copied")
        summed = sem("summed")
        gathered_hi = sem("gathered_hi")
        gathered_lo = sem("gathered_lo")
        zeros_ready = sem("zeros_ready")
        squares_added = sem("squares_added")
        stats_done = sem("stats_done")
        g_mean_ready = sem("g_mean_ready")
        g_rstd_ready = sem("g_rstd_ready")
        silu_ready = sem("silu_ready")
        gu_hi_ready = sem("gu_hi_ready")
        gu_lo_ready = sem("gu_lo_ready")
        down_done = sem("down_done")
        added = sem("added")

        def as_f32(ap):
            return ap.bitcast(F32)

        def landed(eng, u):
            eng.wait_ge(raw_landed[u % RAW], 16 * (u // RAW + 1))

        def pt_blocks(buf, n):
            _, _, i, first, width = keys_of(n)
            j0, nj = first // P, width // P
            at = P * i + PT_STRIDE * j0
            slot = buf[:, n // 4 % 2, :]
            return bass.AP(tensor=slot.tensor, offset=slot.offset + at, ap=[list(slot.ap[0]), [PT_STRIDE, nj], [1, P]])

        def projected(kind, j, part):
            bank = ps[part, PROJ + j % 2, :]
            if kind == "q":
                return bass.AP(tensor=bank.tensor, offset=bank.offset + P - 1, ap=[list(bank.ap[0]), [P, NT], [-1, P]])
            return bank.rearrange("p (t c) -> p t c", c=P)

        def halves(side):
            return tuple(slice(HEAD_DIM * h, HEAD_DIM * (h + 1)) for h in (side, 1 - side))

        def values_hi(slot):
            v = v_both[:, slot, :, :]
            return bass.AP(tensor=v.tensor, offset=v.offset, ap=[list(v.ap[0]), [2 * P, NT], [P + HEAD_DIM, 2], [1, HEAD_DIM]])

        def values_lo(slot):
            return v_both[:, slot, :, HEAD_DIM:HEAD_DIM + P].rearrange("p t (s c) -> p t s c", s=2)

        def out_bank(t, half):
            return ps[:, (PROJ, SCORE)[t % 2] + half, :]

        def by_heads(bank):
            return bank.rearrange("p (t s c) -> p t s c", s=2, c=HEAD_DIM)

        def by_tiles(ap):
            return ap.rearrange("p (t c) -> p t c", c=P)

        def every_row(which):
            return bass.AP(tensor=gains.tensor, offset=which * D_MODEL, ap=[[0, P], [1, D_MODEL]])

        block = ctx.enter_context(nc.Block())

        @block.sync
        def _(sp):
            sp.dma_start(xs[:, 0, :], x[0:P, :]).then_inc(x_landed[0], 16)
            for t in range(1, NT):
                sp.dma_start(xs[:, t, :], x[t * P:(t + 1) * P, :]).then_inc(x_landed[t], 16)
                if t == 1:
                    sp.dma_start(gain[:], every_row(0)).then_inc(gain_landed, 16)
            sp.dma_start(hot, onehot).then_inc(table_landed, 16)
            sp.dma_start(rows, band_add[0:BIAS_HEADS, :]).then_inc(table_landed, 16)
            sp.dma_start(table[:], rel_bias).then_inc(table_landed, 16)
            for e in EVENTS:
                if e[0] == "load":
                    u = e[1]
                    if u == RAW:
                        sp.dma_start(fb[:], f_bias).then_inc(const_landed, 16)
                        sp.dma_start(sink[:], sinks).then_inc(const_landed, 16)
                        sp.dma_start(mix_g[:], mix_gain).then_inc(const_landed, 16)
                        sp.dma_start(pick_f, pick).then_inc(const_landed, 16)
                    if u >= RAW:
                        sp.wait_ge(split_lo, u - RAW + 1)
                    used = NK * F_COLS if u == 0 else UNIT
                    sp.dma_start(raw[:, u % RAW, 0:used], units[u, :, 0:used]).then_inc(raw_landed[u % RAW], 16)
                elif e[0] == "store_rows":
                    sp.wait_ge(rows_ready, 2)
                    sp.dma_start(bias_rows.ap(), rows).then_inc(rows_stored, 16)
                elif e[0] == "bias":
                    pair = e[1]
                    group, step = group_of(pair), 2 if group_of(pair) == GROUP_C else 1
                    if pair < 2:
                        sp.wait_ge(rows_turned, 2 * NT)
                    else:
                        sp.wait_ge(top_ready, 8 * (pair - 1))
                    if group == GROUP_D:
                        src = bass.AP(tensor=band_add.tensor, offset=MASK_ROW * ROW,
                                      ap=[[1, P], [0, 2], [1, SEQ]])
                    else:
                        sp.wait_ge(rows_stored, 16)
                        src = skewed(bias_rows, 4 * (group - 1) + head_of(pair, 0), step)
                    sp.dma_start(tb[:, pair % 2, :].rearrange("p (h c) -> p h c", h=2), src)\
                        .then_inc(bias_landed[pair % 2], 16)
                elif e[0] == "repeat_keys":
                    _, pair, j = e
                    sp.wait_ge(job_hi, hi_upto[j])
                    for side in range(2):
                        own, other = halves(side)
                        sp.dma_start(as_f32(k_twice[other, kv_slot(pair), side, :]),
                                     as_f32(k_twice[own, kv_slot(pair), side, :])).then_inc(keys_repeated, 16)
                elif e[0] == "gain":
                    sp.wait_ge(scaled, NT)
                    sp.dma_start(gain[:], every_row(1)).then_inc(gain_landed, 16)
            with sp.Fori(0, FC // 2) as it:
                for b in range(4):
                    u = U_MLP + b + SPLIT - 1 + RAW
                    sp.wait_ge(split_lo, it * 4 + (u - RAW + 1))
                    sp.dma_start(raw[:, u % RAW, :], units[it * 4 + u]).then_inc(raw_landed[u % RAW], 16)
            sp.wait_ge(scaled, 2 * NT)
            sp.dma_start(gain[:], every_row(2)).then_inc(gain_landed, 16)
            for u in range(U_DOWN + SPLIT - 1 + RAW, N_UNITS):
                sp.wait_ge(split_lo, u - RAW + 1)
                sp.dma_start(raw[:, u % RAW, :], units[u]).then_inc(raw_landed[u % RAW], 16)
            for m in range(2 * NT):
                sp.wait_ge(scaled, 2 * NT + m + 1)
                at = (m // 2, slice(m % 2 * SEQ, (m % 2 + 1) * SEQ))
                sp.dma_start(out[at[0] * P:(at[0] + 1) * P, at[1]], xs[:, at[0], at[1]]).then_inc(out_stored, 16)
            sp.wait_ge(out_stored, 16 * 2 * NT)

        @block.gpsimd
        def _(pool):
            pool.memset(ones[:], 1.0).then_inc(consts_ready, 1)
            pool.memset(ident[:], 0.0).then_inc(consts_ready, 1)
            pool.wait_ge(consts_ready, 2)
            pool.affine_select(out=ident[:], in_=ident[:], compare_op=ALU.not_equal, fill=1.0, base=0,
                               pattern=[[-1, P]], channel_multiplier=1).then_inc(consts_ready, 1)
            pool.memset(mirror[:], 0.0).then_inc(consts_ready, 1)
            pool.wait_ge(consts_ready, 4)
            pool.affine_select(out=mirror[:], in_=mirror[:], compare_op=ALU.not_equal, fill=1.0, base=1 - P,
                               pattern=[[1, P]], channel_multiplier=1).then_inc(consts_ready, 1)
            pool.memset(minus_half[:], -0.5).then_inc(consts_ready, 1)
            pool.memset(as_f32(decay[:]), 0.0).then_inc(consts_ready, 1)
            for buf in (pt_hi, pt_lo):
                pool.memset(as_f32(buf[:, :, 3 * PT_STRIDE + 2 * P:3 * PT_STRIDE + 3 * P]), 0.0).then_inc(consts_ready, 1)
            for e in EVENTS:
                if e[0] == "root":
                    _, which, t = e
                    pool.wait_ge(squared, NT * which + t + 1)
                    pool.tensor_scalar(mean[:, which, t:t + 1], ssq[:, which, t:t + 1], 1.0 / D_MODEL, EPS,
                                       ALU.mult, ALU.add).then_inc(mean_ready, 1)
                    pool.wait_ge(mean_ready, NT * which + t + 1)
                    pool.wait_ge(consts_ready, 6)
                    pool.tensor_tensor(rstd[:, which, t:t + 1], mean[:, which, t:t + 1], minus_half[:, 0:1],
                                       ALU.pow).then_inc(rstd_ready, 1)
                elif e[0] == "norm":
                    n = e[1]
                    width = keys_of(n)[4]
                    pool.wait_ge(inv_ready, n + 1)
                    pool.wait_ge(exp_ready, n + 1)
                    probs = s_buf[:, n % 3, 0:width]
                    pool.tensor_scalar(probs, probs, inv[:, n:n + 1], 1.0, ALU.mult, ALU.mult).then_inc(probs_ready, 1)
                elif e[0] == "values" and e[1] in (10, 11):
                    h = e[1]
                    pool.wait_ge(values_ready, h + 1)
                    for buf in (pt_hi, pt_lo):
                        pool.memset(as_f32(buf[:, h % 2, 2 * P:4 * P]), 0.0).then_inc(zeros_ready, 1)
                elif e[0] == "stats":
                    g = e[1]
                    pool.wait_ge(gathered_hi, 8 * (g + 1))
                    pool.tensor_tensor(sq[:, 0, :], sq[:, 0, :], sq[:, 1, :], ALU.add).then_inc(squares_added, 1)
                elif e[0] == "stats_mean":
                    g = e[1]
                    pool.wait_ge(g_mean_ready, g + 1)
                    pool.tensor_tensor(g_rstd[:, g, :], g_mean[:, g, :], minus_half[:], ALU.pow).then_inc(g_rstd_ready, 1)
            for t in range(NT):
                pool.wait_ge(squared, 2 * NT + 2 * t + 1)
                pool.tensor_scalar(part_mean[:, t:t + 1], ssq_out[:, t, 0:1], 1.0 / D_MODEL, EPS,
                                   ALU.mult, ALU.add).then_inc(mean_ready, 1)
                pool.wait_ge(squared, 2 * NT + 2 * t + 2)
                pool.wait_ge(mean_ready, 2 * NT + 2 * t + 1)
                pool.tensor_scalar(mean[:, 2, t:t + 1], ssq_out[:, t, 1:2], 1.0 / D_MODEL, part_mean[:, t:t + 1],
                                   ALU.mult, ALU.add).then_inc(mean_ready, 1)
                pool.wait_ge(mean_ready, 2 * NT + 2 * t + 2)
                pool.tensor_tensor(rstd[:, 2, t:t + 1], mean[:, 2, t:t + 1], minus_half[:, 0:1],
                                   ALU.pow).then_inc(rstd_ready, 1)

        @block.scalar
        def _(act):
            def split(u):
                landed(act, u)
                if u >= SPLIT and u - SPLIT in UNIT_JOB:
                    act.wait_ge(job_done, UNIT_JOB[u - SPLIT] + 1)
                elif u >= SPLIT:
                    act.wait_ge(out_done, 2 * NT)
                used = NK * F_COLS if u == 0 else UNIT
                act.activation(w_hi[:, u % SPLIT, 0:used], raw[:, u % RAW, 0:used], ACT.Copy).then_inc(split_hi, 1)

            for e in EVENTS:
                if e[0] == "split":
                    split(e[1])
                elif e[0] == "square":
                    _, which, t = e
                    if which == 0:
                        act.wait_ge(x_landed[t], 16)
                    else:
                        act.wait_ge(out_added, 2 * (t + 1))
                    if NT * which + t >= 1:
                        act.wait_ge(squared, NT * which + t)
                    act.activation(ps[:, VALUE:VALUE + 2, :].rearrange("p a b -> p (a b)"), xs[:, t, :], ACT.Square,
                                   accum_out=ssq[:, which, t:t + 1]).then_inc(squared, 1)
                elif e[0] == "drain_h":
                    _, which, t = e
                    for half in range(2):
                        act.wait_ge(rows_turned, 2 * (NT * which + t) + half + 1)
                        if which == 1 and t == 0 and half == 0:
                            act.wait_ge(job_done, job_of["q", PAIRS - 1] + 1)
                        act.activation(h_hi[:, 4 * half:4 * half + 4, t * P:(t + 1) * P],
                                       ps[:, TURN + half, :].rearrange("p (k c) -> p k c", k=4),
                                       ACT.Copy).then_inc(rows_hi, 1)
                elif e[0] == "drain" and e[1] in "qk":
                    _, kind, pair, j = e
                    act.wait_ge(job_done, j + 1)
                    if pair >= 2:
                        act.wait_ge(scores_ready, 8 * (pair - 1))
                    for side in range(2):
                        own, _ = halves(side)
                        dst = q_both[own, pair % 2, side, :] if kind == "q" else k_twice[own, kv_slot(pair), side, :]
                        hi = act.activation(by_tiles(dst), projected(kind, j, own), ACT.Copy,
                                            scale=SCALE if kind == "q" else 1.0)
                    hi.then_inc(job_hi, 1)
                elif e[0] == "decays" and e[1] == 0:
                    act.wait_ge(decay_step, 2)
                    act.activation(s_buf[0:4, 1, :], s_buf[0:4, 1, :], ACT.Exp, scale=-1.0).then_inc(softplus_ready, 1)
                    act.wait_ge(softplus_ready, 1)
                    act.activation(s_buf[0:4, 1, :], s_buf[0:4, 1, :], ACT.Ln, bias=1.0).then_inc(softplus_ready, 1)
                elif e[0] == "drain_v":
                    _, pair, h = e
                    act.wait_ge(values_turned, pair + 1)
                    if pair >= 2:
                        act.wait_ge(values_ready, 2 * (pair - 1))
                    act.activation(values_hi(kv_slot(pair)), by_heads(ps[:, VALUE + h % 2, :]),
                                   ACT.Copy).then_inc(values_hi_ready, 1)
                elif e[0] == "exp":
                    n = e[1]
                    pair, side, i, first, width = keys_of(n)
                    act.wait_ge(shift_ready, n + 1)
                    probs = s_buf[:, n % 3, 0:width]
                    act.activation(probs, probs, ACT.Exp, bias=shift[:, n:n + 1],
                                   accum_out=total[:, n:n + 1]).then_inc(exp_ready, 1)
                    if group_of(pair) == GROUP_C:
                        h = head_of(pair, side)
                        act.activation(sink_e[:, n:n + 1], sink[:, h:h + 1], ACT.Exp,
                                       bias=shift[:, n:n + 1]).then_inc(sink_ready, 1)
                elif e[0] == "keep_hi":
                    n = e[1]
                    width = keys_of(n)[4]
                    act.wait_ge(turned, n + 1)
                    if n >= 8 and n % 4 == 0:
                        act.wait_ge(values_ready, n // 4 - 1)
                    act.activation(pt_blocks(pt_hi, n), ps[:, TURN + n % 2, 0:width].rearrange("p (j c) -> p j c", c=P),
                                   ACT.Copy).then_inc(kept_hi, 1)
                elif e[0] == "sum":
                    h = e[1]
                    own, other = halves(h % 2)
                    act.wait_ge(values_ready, h + 1)
                    if h >= 2:
                        act.wait_ge(gathered_hi, 2 * (h - 1))
                        act.wait_ge(gathered_lo, h - 1)
                    else:
                        act.wait_ge(decay_step, 9)
                    act.activation(head_sum[own, :], ps[other, VALUE + h % 2, :], ACT.Copy).then_inc(low_copied, 1)
                elif e[0] == "gather_hi":
                    h = e[1]
                    pair, r = h // 2, HEAD_DIM * (h % 2)
                    act.wait_ge(summed, h + 1)
                    if pair >= MIX_SLOTS:
                        act.wait_ge(job_done, job_of["out", group_of(pair - MIX_SLOTS), 1, NT - 1] + 1)
                    head_out = head_sum[r:r + HEAD_DIM, :]
                    act.activation(mix_hi[r:r + HEAD_DIM, pair % MIX_SLOTS, :], head_out, ACT.Copy,
                                   scale=mix_g[r:r + HEAD_DIM, pair:pair + 1]).then_inc(gathered_hi, 1)
                    if h >= 4 and h % 4 == 0:
                        act.wait_ge(stats_done, h // 4)
                    act.activation(sq[r:r + HEAD_DIM, pair % 2, :], head_out, ACT.Square).then_inc(gathered_hi, 1)
            with act.Fori(0, FC // 2) as it:
                for b in range(2):
                    for part in range(2):
                        u = U_MLP + 2 * b + part + SPLIT - 1
                        act.wait_ge(raw_landed[u % RAW], it * 16 + 16 * (u // RAW + 1))
                        act.wait_ge(job_done, it * 4 + (JOBS + u - SPLIT - U_MLP + 1))
                        act.activation(w_hi[:, u % SPLIT, :], raw[:, u % RAW, :], ACT.Copy).then_inc(split_hi, 1)
                        if part == 0:
                            act.wait_ge(job_done, it * 4 + (JOBS + 2 * b + 1))
                            act.wait_ge(bank_drained, it * 2 + (JOBS + b - 1))
                            act.activation(act_g[:, b, :], ps[:, PROJ + b, :], ACT.Silu).then_inc(silu_ready, 1)
                    act.wait_ge(bank_drained, it * 2 + (JOBS + b + 1))
                    act.activation(gu_hi[:, it * 2 + b, :], gated[:, b, :], ACT.Copy).then_inc(gu_hi_ready, 1)
            for u in range(U_DOWN + SPLIT - 1, N_UNITS):
                landed(act, u)
                act.wait_ge(job_done, JOBS + u - SPLIT - U_MLP + 1)
                act.activation(w_hi[:, u % SPLIT, :], raw[:, u % RAW, :], ACT.Copy).then_inc(split_hi, 1)
            for m in range(2 * NT):
                t, half = m // 2, m % 2
                act.wait_ge(added, m + 1)
                act.activation(ps[:, m, :], xs[:, t, half * SEQ:(half + 1) * SEQ], ACT.Square,
                               accum_out=ssq_out[:, t, half:half + 1]).then_inc(squared, 1)

        @block.vector
        def _(dve):
            def split(u):
                dve.wait_ge(split_hi, u + 1)
                if u == 0:
                    second = w_hi[:, 0, 0:NK * F_COLS].rearrange("p (k c) -> p k c", c=F_COLS)[:, :, 32:36]
                    dve.tensor_tensor(second, raw[:, 0, 0:NK * F_COLS].rearrange("p (k c) -> p k c", c=F_COLS)[:, :, 32:36],
                                      as_f32(second), ALU.subtract).then_inc(split_lo, 1)
                    return
                dve.tensor_tensor(w_lo[:, u % SPLIT, :], raw[:, u % RAW, :], as_f32(w_hi[:, u % SPLIT, :]),
                                  ALU.subtract).then_inc(split_lo, 1)

            z, soft, log_f, c = (s_buf[0:4, k, :] for k in (0, 1, 2, 0))
            decay_steps = [0]

            def step(ins):
                decay_steps[0] += 1
                ins.then_inc(decay_step, 1)
                dve.wait_ge(decay_step, decay_steps[0])

            for e in EVENTS:
                if e[0] == "split":
                    split(e[1])
                elif e[0] == "scale":
                    _, which, t = e
                    if t >= 2:
                        dve.wait_ge(rows_turned, 2 * (NT * which + t - 1))
                    dve.wait_ge(rstd_ready, NT * which + t + 1)
                    dve.wait_ge(gain_landed, 16 * (which + 1))
                    dve.scalar_tensor_tensor(tb[:, t % 2, :], xs[:, t, :], rstd[:, which, t:t + 1], gain[:], ALU.mult,
                                             ALU.mult).then_inc(scaled, 1)
                elif e[0] == "drain_h":
                    _, which, t = e
                    for half in range(2):
                        ks, ts = slice(4 * half, 4 * half + 4), slice(t * P, (t + 1) * P)
                        dve.wait_ge(rows_hi, 2 * (NT * which + t) + half + 1)
                        dve.tensor_tensor(h_lo[:, ks, ts], ps[:, TURN + half, :].rearrange("p (k c) -> p k c", k=4),
                                          as_f32(h_hi[:, ks, ts]), ALU.subtract).then_inc(rows_kept, 1)
                elif e[0] == "drain_table":
                    dve.wait_ge(table_landed, 48)
                    for part, (at, width) in enumerate(((0, SEQ), (SEQ, ROW - SEQ))):
                        dve.wait_ge(table_done, part + 1)
                        dve.tensor_tensor(rows[:, at:at + width], ps[0:BIAS_HEADS, SCORE + part, 0:width],
                                          rows[:, at:at + width], ALU.add).then_inc(rows_ready, 1)
                elif e[0] == "drain" and e[1] in "qk":
                    _, kind, pair, j = e
                    dve.wait_ge(job_hi, hi_upto[j])
                    for side in range(2):
                        own, other = halves(side)
                        if kind == "q":
                            hi, lo = (q_both[part, pair % 2, side, :] for part in (own, other))
                        else:
                            hi, lo = k_twice[own, kv_slot(pair), side, :], k_lo[own, kv_slot(pair), :]
                        lower = dve.scalar_tensor_tensor(by_tiles(lo), projected(kind, j, own), SCALE if kind == "q" else 1.0,
                                                         by_tiles(as_f32(hi)), ALU.mult, ALU.subtract)
                    lower.then_inc(bank_drained, 1)
                elif e[0] == "drain" and e[1] == "v":
                    _, _, pair, j = e
                    dve.wait_ge(job_done, j + 1)
                    dve.tensor_copy(vt[:], ps[:, PROJ + j % 2, :]).then_inc(bank_drained, 1)
                elif e[0] == "drain" and e[1] == "f":
                    j = e[3]
                    dve.wait_ge(job_done, j + 1)
                    dve.wait_ge(const_landed, 64)
                    dve.wait_ge(rows_stored, 16)
                    step(dve.tensor_scalar(z, ps[0:4, PROJ + j % 2, :], fb[:, 0:1], None, ALU.add))
                    dve.tensor_tensor(z, ps[32:36, PROJ + j % 2, :], z, ALU.add).then_inc(bank_drained, 1)
                    dve.wait_ge(bank_drained, j + 1)
                    step(dve.scalar_tensor_tensor(soft, z, -1.0, z, ALU.mult, ALU.max))
                elif e[0] == "decays" and e[1] == 1:
                    dve.wait_ge(softplus_ready, 2)
                    step(dve.scalar_tensor_tensor(log_f, z, 0.0, soft, ALU.min, ALU.subtract))
                    dve.wait_ge(consts_ready, 9)
                    step(dve.tensor_tensor_scan(c, log_f, as_f32(decay[0:4, :]), 0.0, ALU.add, ALU.add))
                elif e[0] == "decays" and e[1] == 2:
                    step(dve.tensor_scalar(decay[0:4, :], c, -1.0, None, ALU.mult))
                    step(dve.tensor_scalar(decay[64:68, :], c, -1.0, None, ALU.mult))
                elif e[0] == "decays" and e[1] == 3:
                    for r in (32, 96):
                        step(dve.scalar_tensor_tensor(decay[r:r + 4, :], c, -1.0, as_f32(decay[0:4, :]), ALU.mult,
                                                      ALU.subtract))
                    step(dve.tensor_copy(pick_r[:], pick_f))
                elif e[0] == "drain_v":
                    _, pair, h = e
                    slot = kv_slot(pair)
                    dve.wait_ge(values_hi_ready, pair + 1)
                    dve.tensor_tensor(values_lo(slot), by_heads(ps[:, VALUE + h % 2, :]), as_f32(values_hi(slot)),
                                      ALU.subtract).then_inc(values_kept, 1)
                elif e[0] == "max":
                    n = e[1]
                    pair, side, i, first, width = keys_of(n)
                    dve.wait_ge(scores_ready, n + 1)
                    if n % 8 == 0:
                        dve.wait_ge(bias_landed[pair % 2], 16 * (pair // 2 + 1))
                    if n >= 3:
                        dve.wait_ge(turned, n - 2)
                    least = sink[:, head_of(pair, side):head_of(pair, side) + 1] if group_of(pair) == GROUP_C else LOWEST
                    end = SEQ * (side + 1)
                    dve.tensor_tensor_reduce(s_buf[:, n % 3, 0:width], ps[:, SCORE + n % 2, 0:width],
                                             tb[:, pair % 2, end - width:end], 1.0, least, ALU.add, ALU.max,
                                             top[:, n:n + 1]).then_inc(top_ready, 1)
                    dve.wait_ge(top_ready, n + 1)
                    dve.tensor_scalar(shift[:, n:n + 1], top[:, n:n + 1], -1.0, None, ALU.mult).then_inc(shift_ready, 1)
                elif e[0] == "norm":
                    n = e[1]
                    dve.wait_ge(exp_ready, n + 1)
                    sums = total
                    if group_of(n // 8) == GROUP_C:
                        dve.wait_ge(sink_ready, n - 8 * 6 + 1)
                        dve.tensor_tensor(total2[:, n:n + 1], total[:, n:n + 1], sink_e[:, n:n + 1],
                                          ALU.add).then_inc(total_ready, 1)
                        dve.wait_ge(total_ready, n - 8 * 6 + 1)
                        sums = total2
                    dve.reciprocal(inv[:, n:n + 1], sums[:, n:n + 1]).then_inc(inv_ready, 1)
                elif e[0] == "keep_lo":
                    n = e[1]
                    width = keys_of(n)[4]
                    dve.wait_ge(kept_hi, n + 1)
                    dve.tensor_tensor(pt_blocks(pt_lo, n), ps[:, TURN + n % 2, 0:width].rearrange("p (j c) -> p j c", c=P),
                                      as_f32(pt_blocks(pt_hi, n)), ALU.subtract).then_inc(kept_lo, 1)
                elif e[0] == "sum":
                    h = e[1]
                    own, other = halves(h % 2)
                    dve.wait_ge(low_copied, h + 1)
                    dve.tensor_tensor(head_sum[own, :], ps[own, VALUE + h % 2, :], head_sum[own, :],
                                      ALU.add).then_inc(summed, 1)
                elif e[0] == "gather_lo":
                    h = e[1]
                    pair, r = h // 2, HEAD_DIM * (h % 2)
                    dve.wait_ge(gathered_hi, 2 * (h + 1))
                    dve.scalar_tensor_tensor(mix_lo[r:r + HEAD_DIM, pair % MIX_SLOTS, :],
                                             head_sum[r:r + HEAD_DIM, :], mix_g[r:r + HEAD_DIM, pair:pair + 1],
                                             as_f32(mix_hi[r:r + HEAD_DIM, pair % MIX_SLOTS, :]), ALU.mult,
                                             ALU.subtract).then_inc(gathered_lo, 1)
                elif e[0] == "stats_mean":
                    g = e[1]
                    dve.wait_ge(stats_done, g + 1)
                    bank = VALUE if g == GROUP_C else VALUE + 1
                    dve.tensor_scalar(g_mean[:, g, :], by_tiles(ps[:, bank, :])[:, :, 0],
                                      1.0 / (4 * HEAD_DIM), EPS, ALU.mult, ALU.add).then_inc(g_mean_ready, 1)
                elif e[0] == "drain_out":
                    _, g, half, t, j = e
                    cols = slice(half * SEQ, (half + 1) * SEQ)
                    dve.wait_ge(job_done, j + 1)
                    dve.wait_ge(g_rstd_ready, g + 1)
                    dve.wait_ge(bank_drained, j)
                    dve.scalar_tensor_tensor(xs[:, t, cols], ps[:, PROJ + j % 2, :], g_rstd[:, g, t:t + 1],
                                             xs[:, t, cols], ALU.mult, ALU.add).then_inc(bank_drained, 1)
                elif e[0] == "add_c":
                    _, half, t = e
                    cols = slice(half * SEQ, (half + 1) * SEQ)
                    dve.wait_ge(out_done, 2 * t + half + 1)
                    dve.wait_ge(g_rstd_ready, GROUP_C + 1)
                    if t == 0 and half == 0:
                        dve.wait_ge(bank_drained, JOBS)
                    dve.scalar_tensor_tensor(xs[:, t, cols], out_bank(t, half), g_rstd[:, GROUP_C, t:t + 1],
                                             xs[:, t, cols], ALU.mult, ALU.add).then_inc(out_added, 1)
            with dve.Fori(0, FC // 2) as it:
                for b in range(2):
                    for part in range(2):
                        u = U_MLP + 2 * b + part + SPLIT - 1
                        dve.wait_ge(split_hi, it * 4 + (u + 1))
                        dve.tensor_tensor(w_lo[:, u % SPLIT, :], raw[:, u % RAW, :], as_f32(w_hi[:, u % SPLIT, :]),
                                          ALU.subtract).then_inc(split_lo, 1)
                    dve.wait_ge(silu_ready, it * 2 + (b + 1))
                    dve.wait_ge(job_done, it * 4 + (JOBS + 2 * b + 2))
                    dve.tensor_tensor(gated[:, b, :], ps[:, SCORE + b, :], act_g[:, b, :],
                                      ALU.mult).then_inc(bank_drained, 1)
                    dve.wait_ge(gu_hi_ready, it * 2 + (b + 1))
                    dve.tensor_tensor(gu_lo[:, it * 2 + b, :], gated[:, b, :], as_f32(gu_hi[:, it * 2 + b, :]),
                                      ALU.subtract).then_inc(gu_lo_ready, 1)
            for u in range(U_DOWN + SPLIT - 1, N_UNITS):
                split(u)

            def add_down(m):
                at = (slice(None), m // 2, slice(m % 2 * SEQ, (m % 2 + 1) * SEQ))
                dve.wait_ge(down_done, m + 1)
                dve.tensor_tensor(xs[at], ps[:, m, :], xs[at], ALU.add).then_inc(added, 1)

            dve.wait_ge(gain_landed, 16 * 3)
            for t in range(NT + 1):
                if t < NT:
                    add_down(2 * t)
                    add_down(2 * t + 1)
                if t >= 1:
                    dve.wait_ge(rstd_ready, 2 * NT + t)
                    for half in range(2):
                        at = (slice(None), t - 1, slice(half * SEQ, (half + 1) * SEQ))
                        dve.scalar_tensor_tensor(xs[at], xs[at], rstd[:, 2, t - 1:t], gain[:, at[2]], ALU.mult,
                                                 ALU.mult).then_inc(scaled, 1)

        @block.tensor
        def _(pe):
            def thrice(bank, a, b, first, last):
                pe.matmul(bank, a[0], b[0], start=first, stop=False)
                pe.matmul(bank, a[0], b[1], start=False, stop=False)
                return pe.matmul(bank, a[1], b[0], start=False, stop=last)

            def gate_or_up(part, b, u, tokens):
                for k in range(NK):
                    cols = slice(k * P, (k + 1) * P)
                    mm = thrice(ps[:, 2 * part + b, tokens], (w_hi[:, u % SPLIT, cols], w_lo[:, u % SPLIT, cols]),
                                (h_hi[:, k, tokens], h_lo[:, k, tokens]), k == 0, k == NK - 1)
                return mm

            def out_part(u, t, half, c):
                ts, cols, slot = slice(t * P, (t + 1) * P), slice(c * SEQ, (c + 1) * SEQ), (2 * GROUP_C + c) % MIX_SLOTS
                return thrice(out_bank(t, half), (mix_hi[:, slot, ts], mix_lo[:, slot, ts]),
                              (w_hi[:, u % SPLIT, cols], w_lo[:, u % SPLIT, cols]), c == 0, c == 1)

            def values_bank_free(h):
                if h >= 2:
                    pe.wait_ge(summed, h - 1)
                if h % 4 == 1 and h > 4:
                    pe.wait_ge(g_mean_ready, h // 4)

            turned_before = 0

            def bank_free(j):
                if j >= 2:
                    pe.wait_ge(bank_drained, j - 1)

            pe.wait_ge(consts_ready, 1)
            for _ in range(WARM_UP):
                pe.matmul(ps[:, SCORE, 0:P], ones[:], ones[:], start=True, stop=True)
            for e in EVENTS:
                if e[0] == "table":
                    pe.wait_ge(table_landed, 48)
                    for part, (at, width) in enumerate(((0, SEQ), (SEQ, ROW - SEQ))):
                        pe.matmul(ps[0:BIAS_HEADS, SCORE + part, 0:width], table[:], hot[:, at:at + width], start=True,
                                  stop=True).then_inc(table_done, 1)
                elif e[0] == "turn_h":
                    _, which, t = e
                    if which == 0:
                        pe.wait_ge(consts_ready, 3)
                    pe.wait_ge(scaled, NT * which + t + 1)
                    for half in range(2):
                        if NT * which + t >= 1:
                            pe.wait_ge(rows_kept, 2 * (NT * which + t) + half - 1)
                        for k in range(4):
                            at = (4 * half + k) * P
                            mm = pe.transpose(ps[:, TURN + half, k * P:(k + 1) * P], tb[:, t % 2, at:at + P], ident[:])
                        mm.then_inc(rows_turned, 1)
                elif e[0] == "piece":
                    _, kind, u, j, ks, tokens = e
                    if ks[0] == 0:
                        bank_free(j)
                        pe.wait_ge(split_lo, u + 1)
                        pe.wait_ge(rows_kept, 2 * tokens.stop // P)
                    for k in ks if kind == "f" else ():
                        for h in (h_hi, h_lo):
                            mm = pe.matmul(ps[0:F_COLS, PROJ + j % 2, tokens], w_hi[:, 0, k * F_COLS:(k + 1) * F_COLS],
                                           h[:, k, tokens], start=k == 0 and h is h_hi, stop=k == NK - 1 and h is h_lo)
                    for k in ks if kind != "f" else ():
                        cols = slice(k * P, (k + 1) * P)
                        mm = thrice(ps[:, PROJ + j % 2, tokens], (w_hi[:, u % SPLIT, cols], w_lo[:, u % SPLIT, cols]),
                                    (h_hi[:, k, tokens], h_lo[:, k, tokens]), k == 0, k == NK - 1)
                    if ks[-1] == NK - 1 and tokens.stop == SEQ:
                        mm.then_inc(job_done, 1)
                elif e[0] == "turn_v":
                    _, pair, h = e
                    values_bank_free(h)
                    pe.wait_ge(bank_drained, job_of["v", pair] + 1)
                    for t in range(NT):
                        ts = slice(t * P, (t + 1) * P)
                        mm = pe.transpose(ps[:, VALUE + h % 2, ts], vt[:, ts], ident[:])
                    mm.then_inc(values_turned, 1)
                    turned_before = pair + 1
                elif e[0] == "scores":
                    n = e[1]
                    pair, side, i, first, width = keys_of(n)
                    r, qs = slice(HEAD_DIM * side, HEAD_DIM * side + HEAD_DIM), slice(i * P, (i + 1) * P)
                    ks = slice(first, first + max(width, 2 * P))
                    if n % 8 == 0:
                        pe.wait_ge(bank_drained, max(job_of["q", pair], job_of["k", pair]) + 1)
                        pe.wait_ge(keys_repeated, 32 * min(pair + 1, PAIRS - 1))
                    if n == 0:
                        pe.wait_ge(decay_step, 9)
                    if n >= 2:
                        pe.wait_ge(top_ready, n - 1)
                    bank, a, kv = ps[:, SCORE + n % 2, 0:ks.stop - ks.start], pair % 2, kv_slot(pair)
                    of_d = group_of(pair) == GROUP_D
                    pe.matmul(bank, q_both[:, a, side, qs], k_twice[:, kv, side, ks], start=True, stop=False)
                    mm = pe.matmul(bank, q_both[r, a, side, qs], k_lo[r, kv, ks], start=False, stop=not of_d)
                    if of_d:
                        mm = pe.matmul(bank, pick_r[r, head_of(pair, side), :], decay[r, ks], start=False, stop=True)
                    mm.then_inc(scores_ready, 1)
                elif e[0] == "turn":
                    n = e[1]
                    pe.wait_ge(probs_ready, n + 1)
                    if n >= 2:
                        pe.wait_ge(kept_lo, n - 1)
                    for k in range(keys_of(n)[4] // P):
                        ks = slice(k * P, (k + 1) * P)
                        mm = pe.transpose(ps[:, TURN + n % 2, ks], s_buf[:, n % 3, ks], mirror[:])
                    mm.then_inc(turned, 1)
                elif e[0] == "values":
                    h = e[1]
                    pair, side, slot = h // 2, h % 2, kv_slot(h // 2)
                    banded = group_of(pair) == GROUP_C
                    pe.wait_ge(kept_lo, 4 * (h + 1))
                    pe.wait_ge(values_kept, turned_before)
                    values_bank_free(h)
                    if banded and h < 14:
                        pe.wait_ge(zeros_ready, 2 * (h - 11))
                    for k in range(NT):
                        q0, q1 = (min(k, 2), NT if k == 0 or not banded else min(k + 2, NT))
                        moving = slice(PT_STRIDE * k + P * q0, PT_STRIDE * k + P * q1)
                        for which, pt in enumerate((pt_hi, pt_lo)):
                            mm = pe.matmul(ps[:, VALUE + h % 2, P * q0:P * q1], v_both[:, slot, k, P * side:P * (side + 1)],
                                           pt[:, h % 2, moving], start=k == 0 and which == 0,
                                           stop=k == NT - 1 and which == 1)
                    mm.then_inc(values_ready, 1)
                elif e[0] == "stats":
                    g = e[1]
                    pe.wait_ge(summed, 4 * (g + 1))
                    pe.wait_ge(squares_added, g + 1)
                    for t in range(NT):
                        ts = slice(t * P, (t + 1) * P)
                        mm = pe.matmul(ps[:, VALUE + 1, ts], sq[:, 0, ts], ones[:], start=True, stop=True)
                    mm.then_inc(stats_done, 1)
                elif e[0] == "out":
                    _, g, half, t, u, j = e
                    bank_free(j)
                    if t == 0:
                        pe.wait_ge(split_lo, u + 1)
                        pe.wait_ge(gathered_lo, 4 * (g + 1))
                    ts = slice(t * P, (t + 1) * P)
                    for c in range(2):
                        slot, cols = (2 * g + c) % MIX_SLOTS, slice(c * SEQ, (c + 1) * SEQ)
                        mm = thrice(ps[:, PROJ + j % 2, :], (mix_hi[:, slot, ts], mix_lo[:, slot, ts]),
                                    (w_hi[:, u % SPLIT, cols], w_lo[:, u % SPLIT, cols]), c == 0, c == 1)
                    mm.then_inc(job_done, 1)
                elif e[0] == "out_begin":
                    units_c = e[1]
                    pe.wait_ge(bank_drained, JOBS)
                    pe.wait_ge(top_ready, STEPS)
                    pe.wait_ge(gathered_lo, 14)
                    for t in range(2):
                        for half in range(2):
                            if t == 0:
                                pe.wait_ge(split_lo, units_c[half] + 1)
                            out_part(units_c[half], t, half, 0)
                elif e[0] == "stats_end":
                    pe.wait_ge(gathered_hi, 4 * PAIRS)
                    for t in range(NT):
                        ts = slice(t * P, (t + 1) * P)
                        for c in range(2):
                            mm = pe.matmul(ps[:, VALUE, ts], sq[:, c, ts], ones[:], start=c == 0, stop=c == 1)
                    mm.then_inc(stats_done, 1)
                elif e[0] == "out_c":
                    _, half, t, u = e
                    if t >= 2:
                        pe.wait_ge(out_added, 2 * (t - 2) + half + 1)
                        out_part(u, t, half, 0)
                    else:
                        pe.wait_ge(gathered_lo, 2 * PAIRS)
                    out_part(u, t, half, 1).then_inc(out_done, 1)
                elif e[0] == "mlp":
                    _, part, half = e
                    u, tokens = U_MLP + part, slice(half * SEQ // 2, (half + 1) * SEQ // 2)
                    pe.wait_ge(split_lo, u + 1)
                    pe.wait_ge(out_added, 2 * NT)
                    pe.wait_ge(rows_kept, 2 * (NT + tokens.stop // P))
                    mm = gate_or_up(part, 0, u, tokens)
                    if half == 1:
                        mm.then_inc(job_done, 1)

            def features(it, tiles):
                for b in tiles:
                    for part in range(2):
                        u = U_MLP + 2 * b + part
                        pe.wait_ge(split_lo, it * 4 + (u + 1))
                        if part == 0:
                            pe.wait_ge(bank_drained, it * 2 + (JOBS + b - 1))
                        gate_or_up(part, b, u, slice(0, SEQ)).then_inc(job_done, 1)

            features(0, [1])
            with pe.Fori(1, FC // 2) as it:
                features(it, range(2))
            def down(f, t, half):
                ts, cols, u = slice(t * P, (t + 1) * P), slice(half * SEQ, (half + 1) * SEQ), U_DOWN + f
                return thrice(ps[:, 2 * t + half, :], (gu_hi[:, f, ts], gu_lo[:, f, ts]),
                              (w_hi[:, u % SPLIT, cols], w_lo[:, u % SPLIT, cols]), f == 0, f == FC - 1)

            def down_ready(f):
                pe.wait_ge(split_lo, U_DOWN + f + 1)
                pe.wait_ge(gu_lo_ready, f + 1)

            for f in range(FC - TOGETHER):
                down_ready(f)
                for t in range(NT) if f > 0 else (2, 3, 0, 1):
                    if f == 0 and t == 0:
                        pe.wait_ge(bank_drained, JOBS + FC)
                    down(f, t, 0)
                    mm = down(f, t, 1)
                mm.then_inc(job_done, 1)
            for f in range(FC - TOGETHER, FC):
                down_ready(f)
            for m in range(2 * NT):
                for f in range(FC - TOGETHER, FC):
                    mm = down(f, m // 2, m % 2)
                mm.then_inc(down_done, 1)



def weight_units(w_in, w_out, w_gate, w_up, w_down):
    def tiles(w):
        return w.reshape(NK, P, P).transpose(1, 0, 2).reshape(P, UNIT)

    def heads(pair):
        return [head_of(pair, side) for side in range(2)]

    def columns(start, picked):
        return np.concatenate([w_in[:, start + h * HEAD_DIM:start + (h + 1) * HEAD_DIM] for h in picked], axis=1)

    units = {}
    for e in plan()[0]:
        if e[0] == "piece":
            units[e[2]] = (e[1],)
        if e[0] == "out" and e[3] == 0 or e[0] == "out_c" and e[2] == 0:
            g, half, u = (e[1], e[2], e[4]) if e[0] == "out" else (GROUP_C, e[1], e[3])
            rows = []
            for pair in (2 * g, 2 * g + 1):
                at = [MIX_AT[g] + h * HEAD_DIM for h in heads(pair)]
                rows.append(np.concatenate([w_out[a:a + HEAD_DIM, half * SEQ:(half + 1) * SEQ] for a in at]))
            units[u] = np.concatenate(rows, axis=1)
    pending = [u for u in sorted(units) if isinstance(units[u], tuple)]
    seen = {"q": 0, "k": 0, "v": 0}
    for u in pending:
        kind = units[u][0]
        if kind == "f":
            copies = np.zeros((NK, P, F_COLS), np.float32)
            copies[:, :, 0:4] = copies[:, :, 32:36] = w_in[:, F_AT:F_AT + 4].reshape(NK, P, 4)
            units[u] = np.pad(copies.transpose(1, 0, 2).reshape(P, NK * F_COLS), ((0, 0), (0, UNIT - NK * F_COLS)))
            continue
        pair = seen[kind]
        seen[kind] += 1
        g = group_of(pair)
        if kind == "q":
            units[u] = tiles(columns(Q_AT[g], heads(pair)))
        else:
            picked = [0, 1] if g == GROUP_C else heads(pair)
            units[u] = tiles(columns((K_AT if kind == "k" else V_AT)[g], picked))
    out = [units[u] for u in range(len(units))]
    for f in range(FC):
        out += [tiles(w_gate[:, f * P:(f + 1) * P]), tiles(w_up[:, f * P:(f + 1) * P])]
    out += [w_down[f * P:(f + 1) * P, :] for f in range(FC)]
    return np.stack(out)


def kernel(x, norm1_g, w_in, f_bias, sinks, mix_norm_g, w_out, norm2_g, w_gate, w_up, w_down, rel_bias, final_g):
    import concourse.bacc as bacc
    from concourse.bass_utils import run_bass_kernel_spmd

    arrays = [np.asarray(a) for a in (x, norm1_g, w_in, f_bias, sinks, mix_norm_g, w_out, norm2_g, w_gate, w_up,
                                      w_down, rel_bias, final_g)]
    x, norm1_g, w_in, f_bias, sinks, mix_norm_g, w_out, norm2_g, w_gate, w_up, w_down, rel_bias, final_g = arrays
    onehot, band_add, pick = band_constants()
    mix_gain = np.stack([np.concatenate([mix_norm_g[0, MIX_AT[group_of(p)] + h * HEAD_DIM:][:HEAD_DIM]
                                         for h in (head_of(p, 0), head_of(p, 1))]) for p in range(PAIRS)], axis=1)
    ins = {
        "x": x[0],
        "units": weight_units(w_in[0], w_out[0], w_gate[0], w_up[0], w_down[0]),
        "gains": np.stack([norm1_g[0], norm2_g[0], final_g]),
        "mix_gain": mix_gain,
        "f_bias": f_bias.reshape(4, 1),
        "sinks": np.broadcast_to(sinks, (P, 4)),
        "rel_bias": rel_bias,
        "onehot": onehot,
        "band_add": band_add,
        "pick": pick,
    }
    ins = {f"in_{name}": np.ascontiguousarray(a) for name, a in ins.items()}
    nc = bacc.Bacc("TRN2", target_bir_lowering=False, num_devices=1)
    args = [nc.dram_tensor(name, a.shape, mybir.dt.from_np(a.dtype), kind="ExternalInput").ap() for name, a in ins.items()]
    out = nc.dram_tensor("out", (SEQ, D_MODEL), F32, kind="ExternalOutput").ap()
    hybrid_layer(nc, *args, out)
    r = run_bass_kernel_spmd(nc, [ins], core_ids=[0])
    return np.asarray(r.results[0]["out"]).reshape(1, SEQ, D_MODEL)
```
